# Optimizing a Trainium2 kernel written in Bass

```python
import jax, jax.numpy as jnp
from jax import lax
import numpy as np

D_MODEL = 2048
BATCH = 1
SEQ = 256
DEPTH = 2

HEAD_DIM = 128
FOX_HEADS = 8
DSA_HEADS = 8
MLA_HEADS = 8
BRANCH_WIDTH = FOX_HEADS * HEAD_DIM
N_BRANCH = 3
IDX_HEADS = 16
IDX_DIM = 64
TOPK_MAX = 256
Q_LORA = 512
KV_LORA = 512
QK_NOPE = 128
QK_ROPE = 64
V_DIM = 128
ROPE_THETA = 10000.0
BLOCK = 128
EPS = 1e-6

IN_SPLITS = (
    BRANCH_WIDTH, BRANCH_WIDTH, BRANCH_WIDTH, FOX_HEADS,
    BRANCH_WIDTH, BRANCH_WIDTH, BRANCH_WIDTH,
    IDX_HEADS * IDX_DIM, IDX_DIM, IDX_HEADS,
    Q_LORA, KV_LORA, QK_ROPE,
    N_BRANCH * BRANCH_WIDTH,
    N_BRANCH * D_MODEL,
)
D_IN = sum(IN_SPLITS)

kernel_name = 'hybrid_gated_fox_dsa_mla'

def _rmsnorm(x, g):
    xf = x.astype(jnp.float32)
    y = xf * lax.rsqrt(jnp.mean(xf * xf, axis=-1, keepdims=True) + EPS)
    return (y * g.astype(jnp.float32)).astype(x.dtype)

def _rope(x, pos):
    half = x.shape[-1] // 2
    inv = ROPE_THETA ** (-jnp.arange(half, dtype=jnp.float32) / half)
    ang = pos[:, None] * inv[None, :]
    cos = jnp.cos(ang)[:, None, :]
    sin = jnp.sin(ang)[:, None, :]
    xf = x.astype(jnp.float32)
    x1, x2 = xf[..., :half], xf[..., half:]
    return jnp.concatenate([x1 * cos - x2 * sin, x2 * cos + x1 * sin], axis=-1).astype(x.dtype)

def _to_blocks(a):
    b, s = a.shape[:2]
    return jnp.moveaxis(a.reshape((b, s // BLOCK, BLOCK) + a.shape[2:]), 1, 0)

def _from_blocks(a):
    a = jnp.moveaxis(a, 0, 1)
    return a.reshape((a.shape[0], a.shape[1] * a.shape[2]) + a.shape[3:])

def _causal_block_attention(q, k, v, scale, log_cum=None):
    s = q.shape[1]
    key_pos = jnp.arange(s)
    starts = jnp.arange(s // BLOCK) * BLOCK
    cum_k = None if log_cum is None else jnp.moveaxis(log_cum, 1, 2)[:, :, None, :]
    cum_q = None if log_cum is None else _to_blocks(log_cum)

    def one_block(args):
        q_blk, t0, c_blk = args
        logits = jnp.einsum('bthd,bshd->bhts', q_blk, k, preferred_element_type=jnp.float32) * scale
        if c_blk is not None:
            logits = logits + jnp.moveaxis(c_blk, 1, 2)[..., None] - cum_k
        q_pos = t0 + jnp.arange(BLOCK)
        logits = jnp.where(q_pos[:, None] >= key_pos[None, :], logits, -jnp.inf)
        p = jax.nn.softmax(logits, axis=-1)
        return jnp.einsum('bhts,bshd->bthd', p.astype(v.dtype), v)

    return _from_blocks(lax.map(one_block, (_to_blocks(q), starts, cum_q)))

def _dsa_attention(q, k, v, q_idx, k_idx, w_idx, n_sel):
    s = q.shape[1]
    key_pos = jnp.arange(s)
    starts = jnp.arange(s // BLOCK) * BLOCK
    idx_scale = (IDX_HEADS * IDX_DIM) ** -0.5
    attn_scale = HEAD_DIM ** -0.5
    gather = jax.vmap(lambda table, rows: table[rows])

    def one_block(args):
        q_blk, qi_blk, wi_blk, t0 = args
        q_pos = t0 + jnp.arange(BLOCK)
        rel = jax.nn.relu(jnp.einsum('bthe,bse->bths', qi_blk, k_idx, preferred_element_type=jnp.float32))
        score = jnp.einsum('bths,bth->bts', rel, wi_blk.astype(jnp.float32)) * idx_scale
        score = jnp.where(q_pos[:, None] >= key_pos[None, :], score, -jnp.inf)
        _, sel = lax.top_k(score, n_sel)
        k_sel = gather(k, sel)
        v_sel = gather(v, sel)
        logits = jnp.einsum('bthd,btkhd->bhtk', q_blk, k_sel, preferred_element_type=jnp.float32) * attn_scale
        valid = (sel <= q_pos[None, :, None])[:, None]
        p = jax.nn.softmax(jnp.where(valid, logits, -jnp.inf), axis=-1)
        return jnp.einsum('bhtk,btkhd->bthd', p.astype(v.dtype), v_sel)

    return _from_blocks(lax.map(one_block, (_to_blocks(q), _to_blocks(q_idx), _to_blocks(w_idx), starts)))

def _layer(x, pos, n_sel, norm_g, w_in, forget_b, q_norm_g, w_q_up, kv_norm_g, w_kv_up, w_branch, w_out):
    b, s, _ = x.shape
    h = _rmsnorm(x, norm_g)
    z = jnp.einsum('bsd,de->bse', h, w_in)
    points = np.cumsum(IN_SPLITS)[:-1].tolist()
    (f_q, f_k, f_v, f_gate, d_q, d_k, d_v, i_q, i_k, i_w,
     c_q, c_kv, k_pe, silu_g, merge_g) = jnp.split(z, points, axis=-1)

    def heads(t, n):
        return t.reshape(b, s, n, -1)

    log_f = jax.nn.log_sigmoid(f_gate.astype(jnp.float32) + forget_b.astype(jnp.float32))
    cum = jnp.cumsum(log_f, axis=1)
    o_fox = _causal_block_attention(heads(f_q, FOX_HEADS), heads(f_k, FOX_HEADS), heads(f_v, FOX_HEADS),
                                    HEAD_DIM ** -0.5, cum)

    o_dsa = _dsa_attention(_rope(heads(d_q, DSA_HEADS), pos), _rope(heads(d_k, DSA_HEADS), pos),
                           heads(d_v, DSA_HEADS), _rope(heads(i_q, IDX_HEADS), pos),
                           _rope(i_k[:, :, None, :], pos)[:, :, 0], i_w, n_sel)

    q = heads(_rmsnorm(c_q, q_norm_g) @ w_q_up, MLA_HEADS)
    q = jnp.concatenate([q[..., :QK_NOPE], _rope(q[..., QK_NOPE:], pos)], axis=-1)
    kv = heads(_rmsnorm(c_kv, kv_norm_g) @ w_kv_up, MLA_HEADS)
    k_rot = jnp.broadcast_to(_rope(k_pe[:, :, None, :], pos), (b, s, MLA_HEADS, QK_ROPE))
    k = jnp.concatenate([kv[..., :QK_NOPE], k_rot], axis=-1)
    o_mla = _causal_block_attention(q, k, kv[..., QK_NOPE:], (QK_NOPE + QK_ROPE) ** -0.5)

    outs = (o_fox.reshape(b, s, -1), o_dsa.reshape(b, s, -1), o_mla.reshape(b, s, -1))
    gates = jnp.split(silu_g, N_BRANCH, axis=-1)
    merges = jnp.split(merge_g, N_BRANCH, axis=-1)
    terms = [jax.nn.sigmoid(m) * ((o * jax.nn.silu(g)) @ w_branch[i])
             for i, (o, g, m) in enumerate(zip(outs, gates, merges))]
    y = terms[0] + terms[1] + terms[2]
    return x + y @ w_out

def setup_inputs(seed: int = 0) -> dict:
    key = jax.random.key(seed)
    ks = jax.random.split(key, 12)
    nrm = jax.random.normal
    f32 = jnp.float32
    return {
        'x': nrm(ks[0], (BATCH, SEQ, D_MODEL), f32),
        'norm_g': 1.0 + 0.02 * nrm(ks[1], (DEPTH, D_MODEL), f32),
        'w_in': nrm(ks[2], (DEPTH, D_MODEL, D_IN), f32) * D_MODEL ** -0.5,
        'forget_b': 3.0 + 0.5 * nrm(ks[3], (DEPTH, FOX_HEADS), f32),
        'q_norm_g': 1.0 + 0.02 * nrm(ks[4], (DEPTH, Q_LORA), f32),
        'w_q_up': nrm(ks[5], (DEPTH, Q_LORA, MLA_HEADS * (QK_NOPE + QK_ROPE)), f32) * Q_LORA ** -0.5,
        'kv_norm_g': 1.0 + 0.02 * nrm(ks[6], (DEPTH, KV_LORA), f32),
        'w_kv_up': nrm(ks[7], (DEPTH, KV_LORA, MLA_HEADS * (QK_NOPE + V_DIM)), f32) * KV_LORA ** -0.5,
        'w_branch': nrm(ks[8], (DEPTH, N_BRANCH, BRANCH_WIDTH, D_MODEL), f32) * BRANCH_WIDTH ** -0.5,
        'w_out': nrm(ks[9], (DEPTH, D_MODEL, D_MODEL), f32) * D_MODEL ** -0.5,
        'final_norm_g': 1.0 + 0.02 * nrm(ks[10], (D_MODEL,), f32),
    }

def reference(x, norm_g, w_in, forget_b, q_norm_g, w_q_up, kv_norm_g, w_kv_up, w_branch, w_out, final_norm_g):
    s = x.shape[1]
    pos = jnp.arange(s, dtype=jnp.float32)
    n_sel = min(TOPK_MAX, s // 4)
    for l in range(DEPTH):
        x = _layer(x, pos, n_sel, norm_g[l], w_in[l], forget_b[l], q_norm_g[l], w_q_up[l],
                   kv_norm_g[l], w_kv_up[l], w_branch[l], w_out[l])
    return _rmsnorm(x, final_norm_g)


_drawn_inputs = setup_inputs


def setup_inputs(seed=0):
    import zlib

    import numpy as np

    out = dict(_drawn_inputs(seed))
    spreads = {}
    factors = {'norm_g': 3.964, 'q_norm_g': 8.0, 'kv_norm_g': 8.0, 'final_norm_g': 2.866}
    for name, (base, spread) in spreads.items():
        noise = np.random.default_rng([zlib.crc32(name.encode()), seed]).standard_normal(out[name].shape)
        drawn = base * np.exp(spread * noise) if base else spread * noise
        out[name] = __import__('jax').numpy.asarray(drawn.astype(out[name].dtype))
    for name, factor in factors.items():
        out[name] = (out[name] * factor).astype(out[name].dtype)
    return out
```

```python
from contextlib import ExitStack

import numpy as np

import concourse.bass as bass
from concourse import mybir

F32 = mybir.dt.float32
F32R = mybir.dt.float32r
ALU = mybir.AluOpType
ACT = mybir.ActivationFunctionType
AX_X = mybir.AxisListType.X

P = 128
SEQ, D, DEPTH = 256, 2048, 2
TT = SEQ // P
KT = D // P
HEADS, HD = 8, 128
BW = HEADS * HD
IDX_HEADS, IDX_DIM = 16, 64
N_SEL = min(256, SEQ // 4)
LORA, ROPE = 512, 64
LT = LORA // P
QW = HD + ROPE
EPS = 1e-6
NEG = -1e30
TAKEN = -3e38
SCALE = HD ** -0.5
MLA_SCALE = QW ** -0.5
IDX_SCALE = (IDX_HEADS * IDX_DIM) ** -0.5

C_FQ, C_FG = 0, 3 * BW
C_DQ = C_FG + HEADS
C_IQ = C_DQ + 3 * BW
C_IK = C_IQ + IDX_HEADS * IDX_DIM
C_IW = C_IK + IDX_DIM
C_CQ = C_IW + IDX_HEADS
C_CKV = C_CQ + LORA
C_KPE = C_CKV + LORA
C_SILU = C_KPE + ROPE
C_MERGE = C_SILU + 3 * BW
D_IN = C_MERGE + 3 * D
FOX, DSA, MLA = 0, 1, 2

CW = 512
QCW = 2 * QW
N_IK, N_IW, N_KPE, N_FG = 0, 64, 80, 144
NW = N_FG + HEADS
UNITS = 8
RING = 4
TW = P + SEQ

B_NARROW, B_IQ, B_DQ, B_DK, B_DV = 0, 1, 3, 5, 7
B_DG = 9
B_CQ, B_CKV = 17, 18
B_MG0, B_QUP, B_KVUP, B_MG1 = 19, 20, 21, 22
B_FQ, B_FK, B_FV = 29, 31, 33
B_FG = 35
B_OUT = 43
BODIES = 47
U_LAYER = UNITS * BODIES
NARROW_PIECES = 3
RAW_EXTRA = 2 * (NARROW_PIECES - 1) * 16
RAW_LAYER = 16 * 2 * BODIES + RAW_EXTRA


class Order:

    def __init__(self, events, credit=0):
        self.at = {e: i for i, e in enumerate(events)}
        self.layer, self.credit = len(events), credit
        assert len(self.at) == len(events)

    def after(self, l, event):
        return l * self.layer + (self.at[event] + 1 + self.credit)

    def before(self, l, event):
        return l * self.layer + (self.at[event] + self.credit)


class Links:

    def __init__(self, engine, sem, layer):
        self.engine, self.sem, self.layer, self.n = engine, sem, layer, 0

    def __call__(self, l, ins):
        ins.then_inc(self.sem, 1)
        self.n += 1
        self.engine.wait_ge(self.sem, l * self.layer + self.n)

    def close(self):
        assert self.n == self.layer, (self.n, self.layer)


def head_pairs(branch):
    return [(branch, pair) for pair in range(HEADS // 2)]


def attention_fills(branch, pair):
    return [("scores", branch, pair), ("probs", branch, pair)]


X_FILLS = Order(
    [("x", g) for g in range(4)] + [("narrow",), ("cum",), ("iq", 0), ("iq", 1)]
    + [e for b in range(4) for e in (("index", 2 * b), ("qk", DSA, b), ("index", 2 * b + 1))]
    + [e for p in range(4) for e in attention_fills(DSA, p)]
    + [("code", 0), ("code", 1)] + [("q", j) for j in range(4)] + [("k", j) for j in range(3)]
    + [("scores", MLA, 0), ("k", 3), ("probs", MLA, 0)] + [e for p in range(1, 4) for e in attention_fills(MLA, p)]
    + [("qk", FOX, b) for b in range(4)] + [e for p in range(4) for e in attention_fills(FOX, p)]
    + [("y", g) for g in range(4)])
X_CREDIT = 1
PAIRS = Order(head_pairs(DSA) + head_pairs(MLA) + head_pairs(FOX))


def branch_chunks(branch, bank):
    return [("gate", branch, bank)] + [(m, branch, c) for m in ("merge", "proj") for c in range(bank, 4, 2)]


FREED = [
    Order([("v", DSA, 0)] + branch_chunks(DSA, 0) + [("gate", MLA, 0), ("q", 1), ("q", 3), ("k", 1), ("k", 3)]
          + branch_chunks(MLA, 0)[1:] + [("v", FOX, 0)] + branch_chunks(FOX, 0) + [("out", 0), ("out", 2)]),
    Order([("v", DSA, 1)] + branch_chunks(DSA, 1) + [("q", 0), ("q", 2), ("k", 0), ("k", 2)]
          + branch_chunks(MLA, 1) + [("v", FOX, 1)] + branch_chunks(FOX, 1)[:-1] + [("out", 1)]),
]
ROWS = [
    Order([("narrow",), ("iq", 0), ("qk", DSA, 0), ("qk", DSA, 2), ("code", 0), ("q", 0), ("q", 2), ("k", 0),
           ("k", 2), ("qk", FOX, 0), ("qk", FOX, 2)]),
    Order([("iq", 1), ("qk", DSA, 1), ("qk", DSA, 3), ("code", 1), ("q", 1), ("q", 3), ("k", 1), ("k", 3),
           ("qk", FOX, 1), ("qk", FOX, 3)]),
]
NORMS = Order([("x",), ("code", 0), ("code", 1)])
HALVED = Order([("x", g) for g in range(4)] + [("code", 0), ("code", 1)] + [("y", g) for g in range(4)])
TANHS = Order([("gate", b, c) for b in (DSA, MLA, FOX) for c in range(2)])
INDEX_PAIRS = Order([("index", i) for i in range(IDX_HEADS // 2)])
ACT_LINKS, DVE_LINKS = 4, 96


def parity(event):
    return next(i for i in range(2) if event in ROWS[i].at)


def build(nc, x, norm_g, w_in, forget_b, q_norm_g, w_q_up, kv_norm_g, w_kv_up, w_branch, w_out, final_norm_g,
          rope128, rope64, square, negsel, out):
    x_park = nc.dram_tensor("x_park", (P, TT, D), F32).ap()
    with ExitStack() as ctx:
        def sb(name, shape, dt=F32):
            return ctx.enter_context(nc.sbuf_tensor(name, shape, dt))

        def sem(name):
            return ctx.enter_context(nc.semaphore(name))

        raw = sb("raw", [P, RING, 2, CW])
        w_hi = sb("w_hi", [P, RING, 2, CW], F32R)
        w_lo = sb("w_lo", [P, RING, 2, CW], F32R)
        h_hi = sb("h_hi", [P, KT, SEQ], F32R)
        h_lo = sb("h_lo", [P, KT, SEQ], F32R)
        o_hi = sb("o_hi", [P, HEADS, SEQ], F32R)
        o_lo = sb("o_lo", [P, HEADS, SEQ], F32R)
        xy = sb("xy", [P, TT, D])
        qkT = sb("qkT", [P, 2, HEADS, SEQ])
        xs = qkT[:, :, :, :].rearrange("p a h t -> p a (h t)")
        vv = sb("vv", [P, TT, BW])
        gs = sb("gs", [P, TT, BW])
        th = sb("th", [P, TT, D])
        iqT = th[:, 0, :].rearrange("p (b t) -> p b t", b=8)
        junk = th
        ev = sb("ev", [P, TT, CW])
        nat = sb("nat", [P, 2, TT, CW])
        ikT = sb("ikT", [P, SEQ])
        kpT = sb("kpT", [P, SEQ])
        qrT = sb("qrT", [P, HEADS // 2, SEQ])
        score = sb("score", [P, TW])
        dbias = sb("dbias", [P, TW])
        top8 = sb("top8", [P, 2, 8])
        prob = sb("prob", [P, 2, TW])
        probT = sb("probT", [P, 2, TW])
        og = sb("og", [P, 2, TT, HD])
        iw = sb("iw", [P, TT, IDX_HEADS])
        lf = sb("lf", [P, 4, TT, HEADS])
        cumq = sb("cumq", [P, TT, HEADS])
        cumT = sb("cumT", [P, SEQ])
        peak = sb("peak", [P, 2, 2, TT])
        sums = sb("sums", [P, 2, TT])
        rinv = sb("rinv", [P, 2, TT])
        ms = sb("ms", [P, 8, TT])
        rp128 = sb("rp128", [P, 2, TT, HD])
        rp64 = sb("rp64", [P, 2, TT, IDX_DIM])
        sq = sb("sq", [P, 3, P])
        mask = sb("mask", [P, TW])
        ones = sb("ones", [P, P])
        nsel = sb("nsel", [HEADS, HEADS, P])
        g_h = sb("g_h", [P, KT])
        g_c = sb("g_c", [P, 2 * LT])
        fb = sb("fb", [P, HEADS])
        fin_g = gs[:, :, :].rearrange("p a n -> p (a n)")
        ident, tri, diag = sq[:, 0, :], sq[:, 1, :], sq[:, 2, :]

        G = ctx.enter_context(nc.psum_tensor("G", [P, 2, TT, CW], F32))
        X = ctx.enter_context(nc.psum_tensor("X", [P, 2, CW], F32))
        PV = ctx.enter_context(nc.psum_tensor("PV", [P, 2, TT, HD], F32))
        OT = ctx.enter_context(nc.psum_tensor("OT", [P, 2, SEQ], F32))
        XT = X[:, :, :].rearrange("p a n -> p (a n)")

        raw_ready = [sem(f"raw_ready{i}") for i in range(RING)]
        hi_ready = sem("hi_ready")
        unit_split = sem("unit_split")
        unit_done = sem("unit_done")
        freed = [sem("freed0"), sem("freed1")]
        rows_ready = [sem("rows_ready0"), sem("rows_ready1")]
        x_done = sem("x_done")
        x_used = sem("x_used")
        xs_ready = sem("xs_ready")
        y_ready = sem("y_ready")
        x_ready = sem("x_ready")
        hi_taken = sem("hi_taken")
        squared = sem("squared")
        var_ready = sem("var_ready")
        root_ready = sem("root_ready")
        tanh_ready = sem("tanh_ready")
        nope_ready = sem("nope_ready")
        index_used = sem("index_used")
        fabs_ready, flog_ready, logf_ready = sem("fabs_ready"), sem("flog_ready"), sem("logf_ready")
        peak_ready, prob_ready = sem("peak_ready"), sem("prob_ready")
        pv_done, og_ready, ot_done, ot_hi, ot_used = (sem(n) for n in ("pv_done", "og_ready", "ot_done", "ot_hi",
                                                                       "ot_used"))
        x_in, x_parked = sem("x_in"), sem("x_parked")
        consts_in, params_in = sem("consts_in"), sem("params_in")
        mask_ready = sem("mask_ready")
        waited = sem("waited")
        act_link, dve_link = sem("act_link"), sem("dve_link")
        fin_in, out_ready, out_stored = sem("fin_in"), sem("out_ready"), sem("out_stored")

        block = ctx.enter_context(nc.Block())

        w_in_v = w_in.rearrange("l (k p) n -> l p k n", p=P)
        q_up_v = w_q_up.rearrange("l (k p) n -> l p k n", p=P)
        kv_up_v = w_kv_up.rearrange("l (k p) n -> l p k n", p=P)
        br_v = w_branch.rearrange("l b (k p) n -> l b p k n", p=P)
        out_v = w_out.rearrange("l (k p) n -> l p k n", p=P)
        x_v = x.rearrange("a (t p) d -> p (a t) d", p=P)
        o_v = out.rearrange("a (t p) d -> p (a t) d", p=P)
        TILES = ((0, P), (P, TW))

        @block.sync
        def _(sp):
            def load(l, b, p, *pieces):
                sp.wait_ge(unit_split, l * U_LAYER + (UNITS * b + p + 1))
                if p == 0:
                    sp.sem_inc(waited, 1)
                for at, src in pieces:
                    sp.dma_start(raw[:, p % RING, :, at:at + src.shape[-1]], src).then_inc(raw_ready[p % RING], 16)

            def w_in_body(l, b, col):
                for p in range(UNITS):
                    load(l, b, p, (0, w_in_v[l, :, 2 * p:2 * p + 2, col:col + CW]))

            def tail(l, b, branch, first=0):
                for c in range(first, 2):
                    w_in_body(l, b + c - first, C_SILU + branch * BW + c * CW)
                b += 2 - first
                for c in range(4):
                    w_in_body(l, b + c, C_MERGE + branch * D + c * CW)
                for u in range(2 * UNITS):
                    c, k = u // 4, 2 * (u % 4)
                    load(l, b + 4 + u // UNITS, u % UNITS, (0, br_v[l, branch, :, k:k + 2, c * CW:(c + 1) * CW]))

            sp.dma_start(xy[:, :, :], x_v).then_inc(x_in, 16)
            sp.dma_start(rp128[:, :, :, :], rope128).then_inc(consts_in, 16)
            sp.dma_start(rp64[:, :, :, :], rope64).then_inc(consts_in, 16)
            sp.dma_start(sq[:, :, :], square).then_inc(consts_in, 16)
            sp.dma_start(nsel[:, :, :], negsel).then_inc(consts_in, 16)
            with sp.Fori(0, DEPTH) as l:
                sp.wait_ge(y_ready, l + 1)
                sp.dma_start(g_h[:, :], norm_g[l]).then_inc(params_in, 16)
                sp.dma_start(g_c[:, 0:LT], q_norm_g[l]).then_inc(params_in, 16)
                sp.dma_start(g_c[:, LT:2 * LT], kv_norm_g[l]).then_inc(params_in, 16)
                sp.dma_start(fb[:, :], forget_b[l].unsqueeze(0).broadcast_to([P, HEADS])).then_inc(params_in, 16)
                for p in range(UNITS):
                    k = slice(2 * p, 2 * p + 2)
                    load(l, B_NARROW, p, (N_IK, w_in_v[l, :, k, C_IK:C_IK + N_KPE]),
                         (N_KPE, w_in_v[l, :, k, C_KPE:C_KPE + ROPE]), (N_FG, w_in_v[l, :, k, C_FG:C_FG + HEADS]))
                    if p == RING - 1:
                        sp.wait_ge(x_ready, l + 1)
                        sp.dma_start(x_park, xy[:, :, :]).then_inc(x_parked, 16)
                for c in range(2):
                    w_in_body(l, B_IQ + c, C_IQ + c * CW)
                for c in range(6):
                    w_in_body(l, B_DQ + c, C_DQ + c * CW)
                tail(l, B_DG, DSA)
                w_in_body(l, B_CQ, C_CQ)
                w_in_body(l, B_CKV, C_CKV)
                w_in_body(l, B_MG0, C_SILU + MLA * BW)
                for up, b, width in ((q_up_v, B_QUP, QCW), (kv_up_v, B_KVUP, CW)):
                    for p in range(UNITS):
                        c, k = p // 2, 2 * (p % 2)
                        load(l, b, p, (0, up[l, :, k:k + 2, c * width:(c + 1) * width]))
                tail(l, B_MG1, MLA, first=1)
                for c in range(6):
                    w_in_body(l, B_FQ + c, C_FQ + c * CW)
                tail(l, B_FG, FOX)
                for c in range(4):
                    if c == 1:
                        sp.wait_ge(x_done, X_FILLS.after(l, ("y", 3)) )
                        sp.wait_ge(x_parked, 16 * l + 16)
                        sp.dma_start(xy[:, :, :], x_park).then_inc(x_in, 16)
                    for p in range(UNITS):
                        load(l, B_OUT + c, p, (0, out_v[l, :, 2 * p:2 * p + 2, c * CW:(c + 1) * CW]))
            sp.wait_ge(x_ready, DEPTH + 1)
            sp.dma_start(fin_g, final_norm_g.unsqueeze(0).broadcast_to([P, D])).then_inc(fin_in, 16)
            for t in range(TT):
                sp.wait_ge(out_ready, t + 1)
                sp.dma_start(o_v[:, t, :], xy[:, t, :]).then_inc(out_stored, 16)
            sp.wait_ge(out_stored, 16 * TT)

        @block.tensor
        def _(pe):
            def fill(l, event):
                pe.wait_ge(x_used, X_FILLS.before(l, event) + X_CREDIT)

            def units(l, b, width, plan, hi, lo):
                for p in range(UNITS):
                    ks, bank, start, stop, before = plan(p)
                    if start and before in FREED[bank].at:
                        pe.wait_ge(freed[bank], FREED[bank].after(l, before))
                    pe.wait_ge(unit_split, l * U_LAYER + (UNITS * b + p + 1 + RING))
                    for i, k in enumerate(ks):
                        for t in range(TT):
                            dst = G[:, bank, t, 0:width]
                            at = slice(t * P, (t + 1) * P)
                            wh, wl = w_hi[:, p % RING, i, 0:width], w_lo[:, p % RING, i, 0:width]
                            pe.matmul(dst, hi[:, k, at], wh, start=start and i == 0, stop=False)
                            pe.matmul(dst, hi[:, k, at], wl, start=False, stop=False)
                            mm = pe.matmul(dst, lo[:, k, at], wh, start=False, stop=stop and i == 1)
                    mm.then_inc(unit_done, 1)
                    yield p

            def w_in_units(l, b, bank, before, width=CW):
                return units(l, b, width, lambda p: ((2 * p, 2 * p + 1), bank, p == 0, p == UNITS - 1, before),
                             h_hi, h_lo)

            def proj_units(l, b, branch, c0):
                def plan(p):
                    c = c0 + p // 4
                    before = ("merge", branch, c + 2) if c < 2 else ("proj", branch, c - 2)
                    return (2 * (p % 4), 2 * (p % 4) + 1), c % 2, p % 4 == 0, p % 4 == 3, before
                return units(l, b, CW, plan, o_hi, o_lo)

            def up_units(l, b, base, width, before):
                def plan(p):
                    return ((base + 2 * (p % 2), base + 2 * (p % 2) + 1), 1 - p // 2 % 2, p % 2 == 0, p % 2 == 1,
                            before[p // 2])
                return units(l, b, width, plan, o_hi, o_lo)

            def transposes(l, event, blocks):
                i = parity(event)
                pe.wait_ge(rows_ready[i], ROWS[i].after(l, event))
                fill(l, event)
                for j in range(blocks):
                    for t in range(TT):
                        mm = pe.transpose(XT[:, j * SEQ + t * P:j * SEQ + (t + 1) * P],
                                          nat[:, i, t, j * P:(j + 1) * P], ident)
                mm.then_inc(x_done, 1)

            def index_scores(l, pair):
                fill(l, ("index", pair))
                for e in range(2):
                    r = slice(IDX_DIM * e, IDX_DIM * (e + 1))
                    pe.matmul(X[:, e, 0:P], iqT[r, pair, 0:P], ikT[r, 0:P], start=True, stop=True)
                    mm = pe.matmul(X[:, e, P:TW], iqT[r, pair, P:SEQ], ikT[r, :], start=True, stop=True)
                mm.then_inc(x_done, 1)

            def scores(l, branch, pair):
                fill(l, ("scores", branch, pair))
                for e in range(2):
                    h = 2 * pair + e
                    for t, (a, z) in enumerate(TILES):
                        at, keys, dst = slice(t * P, (t + 1) * P), slice(0, (t + 1) * P), X[:, e, a:z]
                        mm = pe.matmul(dst, qkT[:, 0, h, at], qkT[:, 1, h, keys], start=True, stop=branch == DSA)
                        if branch == MLA:
                            r = slice(ROPE * e, ROPE * (e + 1))
                            mm = pe.matmul(dst, qrT[r, pair, at], kpT[r, keys], start=False, stop=True)
                        if branch == FOX:
                            mm = pe.matmul(dst, nsel[:, h, :], cumT[0:HEADS, keys], start=False, stop=True)
                mm.then_inc(x_done, 1)

            def turn_probs(l, branch, pair):
                pe.wait_ge(prob_ready, PAIRS.after(l, (branch, pair)))
                fill(l, ("probs", branch, pair))
                for e in range(2):
                    for j in range(3):
                        mm = pe.transpose(X[:, e, j * P:(j + 1) * P], prob[:, e, j * P:(j + 1) * P], ident)
                mm.then_inc(x_done, 1)

            def values(l, branch, pair):
                pe.wait_ge(x_used, X_FILLS.after(l, ("probs", branch, pair)) + X_CREDIT)
                for e in range(2):
                    h = slice((2 * pair + e) * HD, (2 * pair + e + 1) * HD)
                    pe.matmul(PV[:, e, 0, :], probT[:, e, 0:P], vv[:, 0, h], start=True, stop=True)
                    pe.matmul(PV[:, e, 1, :], probT[:, e, P:2 * P], vv[:, 0, h], start=True, stop=False)
                    mm = pe.matmul(PV[:, e, 1, :], probT[:, e, 2 * P:TW], vv[:, 1, h], start=False, stop=True)
                mm.then_inc(pv_done, 1)

            def turn_heads(l, branch, pair):
                pe.wait_ge(og_ready, PAIRS.after(l, (branch, pair)))
                pe.wait_ge(ot_used, PAIRS.before(l, (branch, pair)) + 1)
                for e in range(2):
                    for t in range(TT):
                        mm = pe.transpose(OT[:, e, t * P:(t + 1) * P], og[:, e, t, :], ident)
                mm.then_inc(ot_done, 1)

            def attend(l, b, branch, first=0):
                for c in range(first, 2):
                    before = ("k", 2) if branch == MLA else ("v", branch, c)
                    for p in w_in_units(l, b, c, before):
                        if branch == MLA and p == 0:
                            transposes(l, ("k", 2), 2)
                        if branch == MLA and p == 3:
                            transposes(l, ("k", 3), 2)
                        if c == 1 and p == 1:
                            scores(l, branch, 0)
                        if c == 1 and p == 5:
                            turn_probs(l, branch, 0)
                    b += 1
                for c in range(4):
                    before = ("merge", branch, c - 2) if c > 1 else ("gate", branch, c)
                    if branch == MLA and c == 0:
                        before = ("k", 3)
                    for p in w_in_units(l, b, c % 2, before):
                        if p == 0:
                            values(l, branch, c)
                        if p == 1 and c < 3:
                            scores(l, branch, c + 1)
                        if p == 3:
                            turn_heads(l, branch, c)
                        if p == 5 and c < 3:
                            turn_probs(l, branch, c + 1)
                    b += 1
                pe.wait_ge(ot_used, PAIRS.after(l, (branch, 3)) + 1)
                for c in (0, 2):
                    for p in proj_units(l, b + c // 2, branch, c):
                        pass

            def turn_width(l, name, src):
                for g in range(4):
                    fill(l, (name, g))
                    for j in range(4):
                        for t in range(TT):
                            k = 4 * g + j
                            mm = pe.transpose(XT[:, j * SEQ + t * P:j * SEQ + (t + 1) * P],
                                              src[:, t, k * P:(k + 1) * P], ident)
                    mm.then_inc(x_done, 1)
                pe.wait_ge(x_used, X_FILLS.after(l, (name, 3)) + X_CREDIT)

            pe.sem_inc(unit_done, RING)
            pe.wait_ge(consts_in, 64)
            with pe.Fori(0, DEPTH) as l:
                pe.wait_ge(xs_ready, l + 1)
                turn_width(l, "x", xs)
                for p in w_in_units(l, B_NARROW, 1, None, NW):
                    pass
                for p in w_in_units(l, B_IQ, 0, None):
                    if p == 3:
                        transposes(l, ("narrow",), 2)
                    if p == 6:
                        pe.wait_ge(logf_ready, l + 1)
                        fill(l, ("cum",))
                        pe.matmul(X[:, 0, 0:HEADS], tri, lf[:, 3, 0, :], start=True, stop=True)
                        pe.matmul(X[:, 0, HEADS:2 * HEADS], ones[:, :], lf[:, 3, 0, :], start=True, stop=False)
                        pe.matmul(X[:, 0, HEADS:2 * HEADS], tri, lf[:, 3, 1, :], start=False, stop=True)
                        pe.matmul(X[0:HEADS, 1, 0:P], lf[:, 3, 0, :], tri, start=True, stop=True)
                        pe.matmul(X[0:HEADS, 1, P:SEQ], lf[:, 3, 0, :], ones[:, :], start=True, stop=False)
                        mm = pe.matmul(X[0:HEADS, 1, P:SEQ], lf[:, 3, 1, :], tri, start=False, stop=True)
                        mm.then_inc(x_done, 1)
                for b in range(B_IQ + 1, B_DG):
                    n = b - B_DQ - 1
                    for p in w_in_units(l, b, (b - B_IQ) % 2, None):
                        if n >= 0 and n < 4 and p == 0:
                            index_scores(l, 2 * n)
                        if n < 4 and p == 3:
                            transposes(l, ("qk", DSA, n) if n >= 0 else ("iq", n + 2), 4)
                        if n >= 0 and n < 4 and p == 5:
                            index_scores(l, 2 * n + 1)
                attend(l, B_DG, DSA)
                for p in w_in_units(l, B_CQ, 0, ("proj", DSA, 2)):
                    pass
                for i, (b, before) in enumerate(((B_CKV, ("proj", DSA, 3)), (B_MG0, None))):
                    for p in w_in_units(l, b, 1 - i, before):
                        if p == 5:
                            transposes(l, ("code", i), 4)
                pe.wait_ge(x_used, X_FILLS.after(l, ("code", 1)) + X_CREDIT)
                for p in up_units(l, B_QUP, 0, QCW, (None, ("gate", MLA, 0), ("q", 0), ("q", 1))):
                    if p == 4 or p == 6:
                        transposes(l, ("q", p // 2 - 2), 3)
                for p in up_units(l, B_KVUP, LT, CW, (("q", 2), ("q", 3), ("k", 0), ("k", 1))):
                    if p == 0 or p == 2:
                        transposes(l, ("q", p // 2 + 2), 3)
                    if p == 4 or p == 6:
                        transposes(l, ("k", p // 2 - 2), 2)
                attend(l, B_MG1, MLA, first=1)
                for b in range(B_FQ, B_FG):
                    n = b - B_FQ - 1
                    before = ("proj", MLA, 2 + n + 1) if n < 1 else None
                    for p in w_in_units(l, b, (b - B_FQ) % 2, before):
                        if 0 <= n < 4 and p == 3:
                            transposes(l, ("qk", FOX, n), 4)
                attend(l, B_FG, FOX)
                pe.wait_ge(y_ready, l + 2)
                turn_width(l, "y", xy)
                for c in range(4):
                    before = ("out", c - 2) if c > 1 else ("proj", FOX, 2 + c)
                    for p in w_in_units(l, B_OUT + c, c % 2, before):
                        pass

        @block.scalar
        def _(act):
            link = Links(act, act_link, ACT_LINKS)

            def units(l, b, width=CW):
                for p in range(UNITS):
                    if b == B_NARROW:
                        n = 16 * NARROW_PIECES * (p // RING + 1)
                    else:
                        n = RAW_EXTRA + 16 * (2 * b + p // RING + 1)
                    act.wait_ge(raw_ready[p % RING], l * RAW_LAYER + n)
                    act.wait_ge(unit_done, l * U_LAYER + (UNITS * b + p + 1))
                    act.copy(w_hi[:, p % RING, :, 0:width], raw[:, p % RING, :, 0:width]).then_inc(hi_ready, 1)
                    yield p

            def chunk_in(l, b, p=UNITS - 1):
                act.wait_ge(unit_done, l * U_LAYER + (UNITS * b + p + 1 + RING))

            def filled(l, event):
                act.wait_ge(x_done, X_FILLS.after(l, event))

            def gate(l, b, branch, c):
                chunk_in(l, b)
                if c:
                    act.wait_ge(freed[0], FREED[0].after(l, ("gate", branch, 0)))
                act.activation(ev[:, :, :], G[:, c, :, :], ACT.Tanh, scale=0.5).then_inc(tanh_ready, 1)

            def merge(l, b, c):
                chunk_in(l, b)
                act.activation(th[:, :, c * CW:(c + 1) * CW], G[:, c % 2, :, :], ACT.Tanh, scale=0.5)\
                   .then_inc(freed[c % 2], 1)

            def softmax(l, branch, pair):
                scale = MLA_SCALE if branch == MLA else SCALE
                act.wait_ge(peak_ready, PAIRS.after(l, (branch, pair)))
                for e in range(2):
                    for t, (a, z) in enumerate(TILES):
                        last = act.activation(prob[:, e, a:z], prob[:, e, a:z], ACT.Exp, scale=scale,
                                              bias=peak[:, 1, e, t:t + 1], accum_out=sums[:, e, t:t + 1])
                last.then_inc(prob_ready, 1)

            def take_probs(l, branch, pair):
                filled(l, ("probs", branch, pair))
                act.copy(probT[:, :, :], X[:, :, 0:TW]).then_inc(x_used, 1)

            def take_heads(l, branch, pair):
                act.wait_ge(ot_done, PAIRS.after(l, (branch, pair)))
                act.copy(o_hi[:, 2 * pair:2 * pair + 2, :], OT[:, :, :]).then_inc(ot_hi, 1)

            def take_values(l, b, bank):
                chunk_in(l, b)
                act.copy(vv[:, :, bank * CW:(bank + 1) * CW], G[:, bank, :, :]).then_inc(freed[bank], 1)

            def latent_kv(l, b, j):
                chunk_in(l, b, 2 * j + 1)
                src = G[:, 1 - j % 2, :, :].rearrange("p t (e c d) -> p t e c d", e=2, c=2)
                for t in range(TT):
                    last = act.copy(nat[:, j % 2, t, 0:2 * HD].rearrange("p (e d) -> p e d", e=2), src[:, t, :, 0, :])
                last.then_inc(rows_ready[j % 2], 1)
                for t in range(TT):
                    last = act.copy(vv[:, t, 2 * j * HD:2 * (j + 1) * HD].rearrange("p (e d) -> p e d", e=2),
                                    src[:, t, :, 1, :])
                last.then_inc(freed[1 - j % 2], 1)

            def take_keys(l, j):
                filled(l, ("k", j))
                act.copy(qkT[:, 1, 2 * j:2 * j + 2, :], X[:, 0, :].rearrange("p (e t) -> p e t", e=2))\
                   .then_inc(x_used, 1)

            def latent_q(l, b, j):
                chunk_in(l, b, 2 * j + 1)
                for t in range(TT):
                    last = act.copy(nat[:, j % 2, t, 0:2 * HD].rearrange("p (e d) -> p e d", e=2),
                                    G[:, 1 - j % 2, t, 0:QCW].rearrange("p (e d) -> p e d", e=2)[:, :, 0:HD])
                last.then_inc(nope_ready, 1)

            def take_queries(l, j):
                filled(l, ("q", j))
                act.copy(qkT[:, 0, 2 * j:2 * j + 2, :], X[:, 0, :].rearrange("p (e t) -> p e t", e=2))
                act.copy(qrT[:, j, :], X[:, 1, 0:SEQ]).then_inc(x_used, 1)

            def take_four(l, event, dst):
                filled(l, event)
                act.copy(dst, X[:, :, :].rearrange("p a (h t) -> p (a h) t", h=2)).then_inc(x_used, 1)

            def attend(l, b, branch, first=0):
                for c in range(first, 2):
                    for p in units(l, b):
                        if branch != MLA and p == 1:
                            if c == 0:
                                take_values(l, b - 1, 1)
                            else:
                                gate(l, b - 1, branch, 0)
                        if branch == MLA and p == 1:
                            take_keys(l, 2)
                            latent_kv(l, b - 1, 3)
                        if c == 1 and p == 4:
                            softmax(l, branch, 0)
                        if branch == MLA and p == 5:
                            take_keys(l, 3)
                        if c == 1 and p == 7:
                            take_probs(l, branch, 0)
                    b += 1
                for c in range(4):
                    for p in units(l, b):
                        if p == 1:
                            if c == 0:
                                gate(l, b - 1, branch, 1)
                            else:
                                merge(l, b - 1, c - 1)
                        if p == 4 and c < 3:
                            softmax(l, branch, c + 1)
                        if p == 5:
                            take_heads(l, branch, c)
                        if p == 7 and c < 3:
                            take_probs(l, branch, c + 1)
                    b += 1
                for c in range(2):
                    for p in units(l, b + c):
                        if c == 0 and p == 1:
                            merge(l, b - 1, 3)

            def root(l, event):
                act.wait_ge(var_ready, NORMS.after(l, event))
                link(l, act.activation(ms[:, 2, :], ms[:, 1, :], ACT.Ln))
                act.activation(ms[:, 3, :], ms[:, 2, :], ACT.Exp, scale=-0.5).then_inc(root_ready, 1)

            def take_upper(l, event, hi, g=None):
                filled(l, event)
                if g is None:
                    last = act.copy(hi, X[:, :, :].rearrange("p a (h t) -> p (a h) t", h=2))
                else:
                    for j in range(4):
                        last = act.activation(hi[:, j, :], XT[:, j * SEQ:(j + 1) * SEQ], ACT.Copy,
                                              scale=g[:, j:j + 1])
                last.then_inc(hi_taken, 1)

            with act.Fori(0, DEPTH) as l:
                for p in units(l, B_NARROW, NW):
                    if p == 1:
                        act.wait_ge(x_ready, l + 1)
                        for t in range(TT):
                            last = act.activation(th[:, t, :], xy[:, t, :], ACT.Square, accum_out=ms[:, 0, t:t + 1])
                        last.then_inc(squared, 1)
                        root(l, ("x",))
                        act.wait_ge(params_in, 64 * l + 64)
                        for g in range(4):
                            take_upper(l, ("x", g), h_hi[:, 4 * g:4 * g + 4, :], g_h[:, 4 * g:4 * g + 4])
                for p in units(l, B_IQ):
                    if p == 3:
                        act.wait_ge(fabs_ready, l + 1)
                        link(l, act.activation(lf[:, 2, :, :], lf[:, 1, :, :], ACT.Exp, scale=-1.0))
                        act.activation(lf[:, 2, :, :], lf[:, 2, :, :], ACT.Ln, bias=1.0).then_inc(flog_ready, 1)
                    if p == 5:
                        filled(l, ("narrow",))
                        act.copy(ikT[:, :], X[:, 0, 0:SEQ])
                        act.copy(kpT[:, :], X[:, 0, SEQ:2 * SEQ]).then_inc(x_used, 1)
                for b in range(B_IQ + 1, B_DG):
                    n = b - B_DQ - 1
                    for p in units(l, b):
                        if b == B_DV + 1 and p == 1:
                            take_values(l, b - 1, 0)
                        if 0 <= n < 4 and (p == 2 or p == 7):
                            pair = 2 * n + (p == 7)
                            filled(l, ("index", pair))
                            act.wait_ge(index_used, INDEX_PAIRS.before(l, ("index", pair)) + 1)
                            act.activation(prob[:, :, :], X[:, :, 0:TW], ACT.Relu).then_inc(x_used, 1)
                        if n < 4 and p == 5:
                            if n < 0:
                                take_four(l, ("iq", n + 2), iqT[:, 4 * (n + 2):4 * (n + 3), :])
                            else:
                                take_four(l, ("qk", DSA, n), qkT[:, n // 2, 4 * (n % 2):4 * (n % 2) + 4, :])
                attend(l, B_DG, DSA)
                for p in units(l, B_CQ):
                    pass
                for i, b in enumerate((B_CKV, B_MG0)):
                    for p in units(l, b):
                        if p == 1:
                            chunk_in(l, b - 1)
                            for t in range(TT):
                                last = act.activation((prob, probT)[t][:, :, 0:CW // 2],
                                                      G[:, i, t, :].rearrange("p (a n) -> p a n", a=2), ACT.Square,
                                                      accum_out=ms[:, 0, t:t + 1])
                            last.then_inc(squared, 1)
                        if p == 3:
                            root(l, ("code", i))
                        if p == 7:
                            take_upper(l, ("code", i), o_hi[:, LT * i:LT * (i + 1), :], g_c[:, LT * i:LT * (i + 1)])
                for p in units(l, B_QUP, QCW):
                    if p == 1:
                        gate(l, B_MG0, MLA, 0)
                    if p in (3, 5, 7):
                        latent_q(l, B_QUP, (p - 3) // 2)
                    if p == 6:
                        take_queries(l, 0)
                for p in units(l, B_KVUP):
                    if p == 0 or p == 2 or p == 4:
                        take_queries(l, 1 + p // 2)
                    if p == 1:
                        latent_q(l, B_QUP, 3)
                    if p == 3 or p == 5:
                        latent_kv(l, B_KVUP, (p - 3) // 2)
                    if p == 6:
                        take_keys(l, 0)
                    if p == 7:
                        latent_kv(l, B_KVUP, 2)
                        take_keys(l, 1)
                attend(l, B_MG1, MLA, first=1)
                for b in range(B_FQ, B_FG):
                    n = b - B_FQ - 1
                    for p in units(l, b):
                        if 0 <= n < 4 and p == 1:
                            chunk_in(l, b - 1)
                            act.copy(nat[:, n % 2, :, :], G[:, n % 2, :, :]).then_inc(rows_ready[n % 2], 1)
                        if n == 4 and p == 1:
                            take_values(l, b - 1, 0)
                        if 0 <= n < 4 and p == 5:
                            take_four(l, ("qk", FOX, n), qkT[:, n // 2, 4 * (n % 2):4 * (n % 2) + 4, :])
                attend(l, B_FG, FOX)
                for b in range(B_OUT, BODIES):
                    for p in units(l, b):
                        if b == B_OUT and p == 1:
                            for g in range(4):
                                take_upper(l, ("y", g), h_hi[:, 4 * g:4 * g + 4, :])
                link.close()
            act.wait_ge(x_ready, DEPTH + 1)
            for t in range(TT):
                last = act.activation(th[:, t, :], xy[:, t, :], ACT.Square, accum_out=ms[:, 0, t:t + 1])
            last.then_inc(squared, 1)
            act.wait_ge(var_ready, NORMS.layer * DEPTH + 1)
            act.activation(ms[:, 2, :], ms[:, 1, :], ACT.Ln).then_inc(act_link, 1)
            act.wait_ge(act_link, ACT_LINKS * DEPTH + 1)
            act.activation(ms[:, 3, :], ms[:, 2, :], ACT.Exp, scale=-0.5).then_inc(root_ready, 1)

        @block.vector
        def _(dve):
            link = Links(dve, dve_link, DVE_LINKS)

            def units(l, b, width=CW):
                for p in range(UNITS):
                    dve.wait_ge(hi_ready, l * U_LAYER + (UNITS * b + p + 1))
                    r = p % RING
                    dve.tensor_tensor(w_lo[:, r, :, 0:width], raw[:, r, :, 0:width],
                                      w_hi[:, r, :, 0:width].bitcast(F32), ALU.subtract).then_inc(unit_split, 1)
                    yield p

            def chunk_in(l, b, p=UNITS - 1):
                dve.wait_ge(unit_done, l * U_LAYER + (UNITS * b + p + 1 + RING))

            def filled(l, event):
                dve.wait_ge(x_done, X_FILLS.after(l, event))

            def rotate(l, t1, src, dst, table, heads, dim):
                half = dim // 2
                for t in range(TT):
                    cos = table[:, 0, t, :].unsqueeze(1).broadcast_to([P, heads, dim])
                    dve.tensor_tensor(t1[:, t], src[:, t], cos, ALU.mult)
                    sin = table[:, 1, t, :].unsqueeze(1).broadcast_to([P, heads, dim])
                    dve.tensor_tensor(dst[:, t, :, 0:half], src[:, t, :, half:dim], sin[:, :, 0:half], ALU.mult)
                    last = dve.tensor_tensor(dst[:, t, :, half:dim], src[:, t, :, 0:half], sin[:, :, half:dim],
                                             ALU.mult)
                return last

            def rotate_chunk(l, b, bank, i, table, heads, dim):
                chunk_in(l, b)
                src = G[:, bank, :, :].rearrange("p t (h d) -> p t h d", h=heads)
                t1 = ev[:, :, :].rearrange("p t (h d) -> p t h d", h=heads)
                dst = nat[:, i, :, :].rearrange("p t (h d) -> p t h d", h=heads)
                link(l, rotate(l, t1, src, dst, table, heads, dim))
                dve.tensor_tensor(nat[:, i, :, :], nat[:, i, :, :], ev[:, :, :], ALU.add).then_inc(rows_ready[i], 1)

            def norm_factor(l, event, width):
                dve.wait_ge(squared, NORMS.after(l, event))
                dve.tensor_scalar(ms[:, 1, :], ms[:, 0, :], 1.0 / width, EPS, ALU.mult, ALU.add)\
                   .then_inc(var_ready, 1)

            def newton(l, event, link=link):
                dve.wait_ge(root_ready, NORMS.after(l, event))
                link(l, dve.tensor_tensor(ms[:, 4, :], ms[:, 3, :], ms[:, 3, :], ALU.mult))
                link(l, dve.tensor_tensor(ms[:, 5, :], ms[:, 4, :], ms[:, 1, :], ALU.mult))
                link(l, dve.tensor_scalar(ms[:, 6, :], ms[:, 5, :], -0.5, 1.5, ALU.mult, ALU.add))
                link(l, dve.tensor_tensor(ms[:, 7, :], ms[:, 3, :], ms[:, 6, :], ALU.mult))

            def take_lower(l, event, hi, lo, g=None):
                dve.wait_ge(hi_taken, HALVED.after(l, event))
                filled(l, event)
                if g is None:
                    last = dve.tensor_tensor(lo, X[:, :, :].rearrange("p a (h t) -> p (a h) t", h=2),
                                             hi.bitcast(F32), ALU.subtract)
                else:
                    for j in range(4):
                        last = dve.scalar_tensor_tensor(out=lo[:, j, :], in0=XT[:, j * SEQ:(j + 1) * SEQ],
                                                        scalar=g[:, j:j + 1], in1=hi[:, j, :].bitcast(F32),
                                                        op0=ALU.mult, op1=ALU.subtract)
                last.then_inc(x_used, 1)

            def gate(l, branch, c):
                dve.wait_ge(tanh_ready, TANHS.after(l, ("gate", branch, c)))
                dve.scalar_tensor_tensor(out=gs[:, :, c * CW:(c + 1) * CW], in0=ev[:, :, :], scalar=1.0,
                                         in1=G[:, c, :, :], op0=ALU.add, op1=ALU.mult).then_inc(freed[c], 1)

            def logits(l, branch, pair):
                filled(l, ("scores", branch, pair))
                if branch == FOX:
                    for e in range(2):
                        for t, (a, z) in enumerate(TILES):
                            h = 2 * pair + e
                            last = dve.scalar_tensor_tensor(out=prob[:, e, a:z], in0=X[:, e, a:z],
                                                            scalar=cumq[:, t, h:h + 1], in1=mask[:, a:z],
                                                            op0=ALU.add, op1=ALU.add)
                else:
                    bias = dbias if branch == DSA else mask
                    last = dve.tensor_tensor(prob[:, :, :], X[:, :, 0:TW],
                                             bias[:, :].unsqueeze(1).broadcast_to([P, 2, TW]), ALU.add)
                last.then_inc(x_used, 1)
                dve.wait_ge(x_used, X_FILLS.after(l, ("scores", branch, pair)) + X_CREDIT)
                for t, (a, z) in enumerate(TILES):
                    last = dve.tensor_reduce(peak[:, 0, :, t], prob[:, :, a:z], AX_X, ALU.max)
                link(l, last)
                scale = MLA_SCALE if branch == MLA else SCALE
                dve.tensor_scalar(peak[:, 1, :, :], peak[:, 0, :, :], -scale, None, ALU.mult).then_inc(peak_ready, 1)

            def gate_heads(l, branch, pair):
                dve.wait_ge(prob_ready, PAIRS.after(l, (branch, pair)))
                link(l, dve.reciprocal(rinv[:, :, :], sums[:, :, :]))
                link(l, dve.tensor_scalar(rinv[:, :, :], rinv[:, :, :], 0.5, None, ALU.mult))
                dve.wait_ge(pv_done, PAIRS.after(l, (branch, pair)))
                for e in range(2):
                    h = slice((2 * pair + e) * HD, (2 * pair + e + 1) * HD)
                    for t in range(TT):
                        last = dve.scalar_tensor_tensor(out=og[:, e, t, :], in0=PV[:, e, t, :],
                                                        scalar=rinv[:, e, t:t + 1], in1=gs[:, t, h],
                                                        op0=ALU.mult, op1=ALU.mult)
                last.then_inc(og_ready, 1)

            def rest_of_heads(l, branch, pair):
                dve.wait_ge(ot_hi, PAIRS.after(l, (branch, pair)))
                at = slice(2 * pair, 2 * pair + 2)
                dve.tensor_tensor(o_lo[:, at, :], OT[:, :, :], o_hi[:, at, :].bitcast(F32), ALU.subtract)\
                   .then_inc(ot_used, 1)

            def project(l, b, branch, c):
                chunk_in(l, b, 4 * (c % 2) + 3)
                if branch == DSA and c == 0:
                    dve.wait_ge(x_parked, 16 * l + 16)
                at = slice(c * CW, (c + 1) * CW)
                link(l, dve.scalar_tensor_tensor(out=ev[:, :, :], in0=th[:, :, at], scalar=1.0, in1=G[:, c % 2, :, :],
                                                 op0=ALU.add, op1=ALU.mult))
                if branch == DSA:
                    last = dve.tensor_scalar(xy[:, :, at], ev[:, :, :], 0.5, None, ALU.mult)
                else:
                    last = dve.scalar_tensor_tensor(out=xy[:, :, at], in0=ev[:, :, :], scalar=0.5, in1=xy[:, :, at],
                                                    op0=ALU.mult, op1=ALU.add)
                last.then_inc(y_ready if branch == FOX and c == 3 else freed[c % 2], 1)

            def attend(l, b, branch, first=0):
                for c in range(first, 2):
                    for p in units(l, b):
                        if branch == DSA and c == 0 and p == 2:
                            link(l, dve.tensor_scalar(dbias[:, :], score[:, :], TAKEN / 1.5, NEG, ALU.is_gt, ALU.mult))
                            link(l, dve.tensor_tensor(dbias[:, :], dbias[:, :], mask[:, :], ALU.add))
                        if branch != MLA and c == 1 and p == 1:
                            gate(l, branch, 0)
                        if c == 1 and p == 3:
                            logits(l, branch, 0)
                    b += 1
                for c in range(4):
                    for p in units(l, b):
                        if c == 0 and p == 1:
                            gate(l, branch, 1)
                        if p == 2:
                            gate_heads(l, branch, c)
                        if p == 3 and c < 3:
                            logits(l, branch, c + 1)
                        if p == 5:
                            rest_of_heads(l, branch, c)
                    b += 1
                for c in range(2):
                    for p in units(l, b + c):
                        if c == 1 and p == 1:
                            project(l, b, branch, 1)
                        if p == 5:
                            project(l, b + c, branch, 2 * c)

            def latent_q(l, b, j):
                dve.wait_ge(nope_ready, l * 4 + (j + 1))
                chunk_in(l, b, 2 * j + 1)
                src = G[:, 1 - j % 2, :, 0:QCW].rearrange("p t (e d) -> p t e d", e=2)[:, :, :, HD:QW]
                dst = nat[:, j % 2, :, 2 * HD:3 * HD].rearrange("p t (e d) -> p t e d", e=2)
                t1 = ev[:, :, 0:HD].rearrange("p t (e d) -> p t e d", e=2)
                if j:
                    dve.wait_ge(rows_ready[(j - 1) % 2], ROWS[(j - 1) % 2].after(l, ("q", j - 1)))
                else:
                    dve.wait_ge(freed[0], FREED[0].after(l, ("gate", MLA, 0)))
                rotate(l, t1, src, dst, rp64, 2, ROPE).then_inc(freed[1 - j % 2], 1)
                dve.wait_ge(freed[1 - j % 2], FREED[1 - j % 2].after(l, ("q", j)))
                dve.tensor_tensor(nat[:, j % 2, :, 2 * HD:3 * HD], nat[:, j % 2, :, 2 * HD:3 * HD], ev[:, :, 0:HD],
                                  ALU.add).then_inc(rows_ready[j % 2], 1)

            dve.sem_inc(unit_split, RING)
            dve.sem_inc(x_used, X_CREDIT)
            for free in (ot_used, index_used, y_ready):
                dve.sem_inc(free, 1)
            dve.memset(ones[:, :], 1.0)
            dve.memset(ms[:, :, :], 1.0)
            dve.wait_ge(consts_in, 64)
            dve.tensor_scalar(mask[:, 0:P], diag, 1.0, None, ALU.mult)
            dve.tensor_scalar(mask[:, P:2 * P], diag, 0.0, None, ALU.mult)
            dve.tensor_scalar(mask[:, 2 * P:TW], diag, 1.0, None, ALU.mult).then_inc(mask_ready, 1)
            dve.wait_ge(mask_ready, 1)
            dve.wait_ge(x_in, 16)
            dve.sem_inc(x_ready, 1)
            with dve.Fori(0, DEPTH) as l:
                for p in units(l, B_NARROW, NW):
                    if p == 1:
                        norm_factor(l, ("x",), D)
                        newton(l, ("x",))
                        for t in range(TT):
                            last = dve.tensor_scalar(xs[:, t, :], xy[:, t, :], ms[:, 7, t:t + 1], None, ALU.mult)
                        last.then_inc(xs_ready, 1)
                        dve.wait_ge(params_in, 64 * l + 64)
                        for g in range(4):
                            at = slice(4 * g, 4 * g + 4)
                            take_lower(l, ("x", g), h_hi[:, at, :], h_lo[:, at, :], g_h[:, at])
                for p in units(l, B_IQ):
                    if p == 1:
                        chunk_in(l, B_NARROW)
                        z = G[:, 1, :, :]
                        dve.tensor_scalar(iw[:, :, :], z[:, :, N_IW:N_KPE], IDX_SCALE, None, ALU.mult)
                        link(l, dve.tensor_tensor(lf[:, 0, :, :], z[:, :, N_FG:NW],
                                                  fb[:, :].unsqueeze(1).broadcast_to([P, TT, HEADS]), ALU.add))
                        src = z[:, :, 0:2 * N_KPE].rearrange("p t (e d) -> p t e d", e=2)[:, :, :, 0:ROPE]
                        dup = nat[:, 0, :, 0:2 * P].rearrange("p t (e c d) -> p t e c d", e=2, c=2)
                        t1 = ev[:, :, 0:P].rearrange("p t (e d) -> p t e d", e=2)
                        link(l, rotate(l, t1, src, dup[:, :, :, 0, :], rp64, 2, ROPE))
                        for t in range(TT):
                            dve.tensor_tensor(dup[:, t, :, 1, :], dup[:, t, :, 0, :], t1[:, t], ALU.add)
                        for t in range(TT):
                            last = dve.tensor_tensor(dup[:, t, :, 0, :], dup[:, t, :, 0, :], t1[:, t], ALU.add)
                        last.then_inc(rows_ready[0], 1)
                    if p == 2:
                        link(l, dve.tensor_scalar(lf[:, 1, :, :], lf[:, 0, :, :], -1.0, None, ALU.mult))
                        dve.tensor_tensor(lf[:, 1, :, :], lf[:, 1, :, :], lf[:, 0, :, :], ALU.max)\
                           .then_inc(fabs_ready, 1)
                    if p == 4:
                        dve.wait_ge(flog_ready, l + 1)
                        dve.scalar_tensor_tensor(out=lf[:, 3, :, :], in0=lf[:, 0, :, :], scalar=0.0,
                                                 in1=lf[:, 2, :, :], op0=ALU.min, op1=ALU.subtract)\
                           .then_inc(logf_ready, 1)
                    if p == 7:
                        filled(l, ("cum",))
                        dve.tensor_scalar(cumq[:, :, :], X[:, 0, 0:2 * HEADS].rearrange("p (t h) -> p t h", t=TT),
                                          1 / SCALE, None, ALU.mult)
                        dve.tensor_scalar(cumT[0:HEADS, :], X[0:HEADS, 1, 0:SEQ], 1 / SCALE, None, ALU.mult)\
                           .then_inc(x_used, 1)
                for b in range(B_IQ + 1, B_DG):
                    n = b - B_DQ - 1
                    for p in units(l, b):
                        if b == B_DV + 1:
                            if p == 0:
                                link(l, dve.tensor_tensor(score[:, :], score[:, :], mask[:, :], ALU.add))
                            dve.sem_inc(waited, 1)
                            for t, (a, z) in enumerate(TILES):
                                last = dve.max(top8[:, t, :], score[:, a:z])
                            link(l, last)
                            dve.sem_inc(waited, 1)
                            for t, (a, z) in enumerate(TILES):
                                last = dve.match_replace(score[:, a:z], top8[:, t, :], score[:, a:z], TAKEN)
                            link(l, last)
                        if n < 0 and p == 1:
                            rotate_chunk(l, b - 1, n + 2, n + 2, rp64, 8, IDX_DIM)
                        if 0 <= n < 4 and p == 1:
                            rotate_chunk(l, b - 1, n % 2, n % 2, rp128, 4, HD)
                        if 0 <= n < 4 and (p == 2 or p == 7):
                            pair = 2 * n + (p == 7)
                            dve.wait_ge(x_used, X_FILLS.after(l, ("index", pair)) + X_CREDIT)
                            for e in range(2):
                                for t, (a, z) in enumerate(TILES):
                                    w = iw[:, t, 2 * pair + e:2 * pair + e + 1]
                                    if pair == 0 and e == 0:
                                        last = dve.tensor_scalar(score[:, a:z], prob[:, e, a:z], w, None, ALU.mult)
                                    else:
                                        last = dve.scalar_tensor_tensor(out=score[:, a:z], in0=prob[:, e, a:z],
                                                                        scalar=w, in1=score[:, a:z], op0=ALU.mult,
                                                                        op1=ALU.add)
                                if e == 0:
                                    link(l, last)
                            last.then_inc(index_used, 1)
                            dve.wait_ge(index_used, INDEX_PAIRS.after(l, ("index", pair)) + 1)
                attend(l, B_DG, DSA)
                for p in units(l, B_CQ):
                    if p == 1:
                        project(l, B_CQ - 1, DSA, 3)
                for i, b in enumerate((B_CKV, B_MG0)):
                    for p in units(l, b):
                        if p == 2:
                            norm_factor(l, ("code", i), LORA)
                        if p == 4:
                            newton(l, ("code", i))
                            for t in range(TT):
                                last = dve.tensor_scalar(nat[:, i, t, :], G[:, i, t, :], ms[:, 7, t:t + 1], None,
                                                         ALU.mult)
                            last.then_inc(rows_ready[i], 1)
                        if p == 7:
                            at = slice(LT * i, LT * (i + 1))
                            take_lower(l, ("code", i), o_hi[:, at, :], o_lo[:, at, :], g_c[:, at])
                for p in units(l, B_QUP, QCW):
                    if p == 1:
                        gate(l, MLA, 0)
                    if p in (3, 5, 7):
                        latent_q(l, B_QUP, (p - 3) // 2)
                for p in units(l, B_KVUP):
                    if p == 1:
                        latent_q(l, B_QUP, 3)
                attend(l, B_MG1, MLA, first=1)
                for b in range(B_FQ, B_FG):
                    for p in units(l, b):
                        if b == B_FQ and p == 1:
                            project(l, B_FQ - 1, MLA, 3)
                attend(l, B_FG, FOX)
                for c in range(4):
                    for p in units(l, B_OUT + c):
                        if c == 0 and p == 1:
                            project(l, B_OUT - 1, FOX, 3)
                            for g in range(4):
                                at = slice(4 * g, 4 * g + 4)
                                take_lower(l, ("y", g), h_hi[:, at, :], h_lo[:, at, :])
                        if c and p == 1:
                            if c == 1:
                                dve.wait_ge(x_in, 16 * l + 32)
                            chunk_in(l, B_OUT + c - 1)
                            at = slice((c - 1) * CW, c * CW)
                            dve.tensor_tensor(xy[:, :, at], G[:, (c - 1) % 2, :, :], xy[:, :, at], ALU.add)\
                               .then_inc(freed[(c - 1) % 2], 1)
                chunk_in(l, BODIES - 1)
                dve.tensor_tensor(xy[:, :, 3 * CW:D], G[:, 1, :, :], xy[:, :, 3 * CW:D], ALU.add).then_inc(x_ready, 1)
                link.close()
            dve.wait_ge(squared, NORMS.layer * DEPTH + 1)
            dve.tensor_scalar(ms[:, 1, :], ms[:, 0, :], 1.0 / D, EPS, ALU.mult, ALU.add).then_inc(var_ready, 1)
            last_links = Links(dve, dve_link, DVE_LINKS)
            newton(DEPTH, ("x",), last_links)
            dve.wait_ge(fin_in, 16)
            for t in range(TT):
                dve.scalar_tensor_tensor(out=xy[:, t, :], in0=xy[:, t, :], scalar=ms[:, 7, t:t + 1], in1=fin_g,
                                         op0=ALU.mult, op1=ALU.mult).then_inc(out_ready, 1)


_INS = ["x", "norm_g", "w_in", "forget_b", "q_norm_g", "w_q_up", "kv_norm_g", "w_kv_up", "w_branch", "w_out",
        "final_norm_g"]


def rope_table(dim):
    half = dim // 2
    inv = np.float32(10000.0) ** (-np.arange(half, dtype=np.float32) / np.float32(half))
    ang = np.arange(SEQ, dtype=np.float32)[:, None] * inv[None, :].astype(np.float32)
    cos, sin = np.cos(ang), np.sin(ang)
    both = np.stack([np.concatenate([cos, cos], 1), np.concatenate([-sin, sin], 1)], 1)
    return np.ascontiguousarray(both.reshape(TT, P, 2, dim).transpose(1, 2, 0, 3).astype(np.float32))


def kernel(**inputs):
    import concourse.bacc as bacc
    from concourse.bass_utils import run_bass_kernel_spmd

    nc = bacc.Bacc("TRN2", target_bir_lowering=False, num_devices=1)
    r = np.arange(P)
    square = np.stack([r[:, None] == r[None, :], r[:, None] <= r[None, :],
                       np.where(r[:, None] < r[None, :], NEG, 0.0)], 1).astype(np.float32)
    negsel = -np.repeat(np.eye(HEADS, dtype=np.float32)[:, :, None], P, 2)
    given = {n: np.ascontiguousarray(inputs[n]) for n in _INS}
    for n in ("norm_g", "q_norm_g", "kv_norm_g"):
        given[n] = np.ascontiguousarray(given[n].reshape(DEPTH, -1, P).transpose(0, 2, 1))
    given.update(rope128=rope_table(HD), rope64=rope_table(ROPE), square=square,
                 negsel=np.ascontiguousarray(negsel))
    args = {n: nc.dram_tensor(f"in_{n}", a.shape, F32, kind="ExternalInput").ap() for n, a in given.items()}
    out = nc.dram_tensor("out", (1, SEQ, D), F32, kind="ExternalOutput").ap()
    build(nc, out=out, **args)
    r = run_bass_kernel_spmd(nc, [{f"in_{n}": a for n, a in given.items()}], core_ids=[0])
    return r.results[0]["out"]
```

```python
from contextlib import ExitStack

import numpy as np

import concourse.bass as bass
from concourse import mybir

F32 = mybir.dt.float32
F32R = mybir.dt.float32r
ALU = mybir.AluOpType
ACT = mybir.ActivationFunctionType
AX_X = mybir.AxisListType.X

P = 128
SEQ, D, DEPTH = 256, 2048, 2
TT = SEQ // P
KT = D // P
HEADS, HD = 8, 128
BW = HEADS * HD
IDX_HEADS, IDX_DIM = 16, 64
N_SEL = min(256, SEQ // 4)
LORA, ROPE = 512, 64
LT = LORA // P
QW = HD + ROPE
EPS = 1e-6
NEG = -1e30
TAKEN = -3e38
SCALE = HD ** -0.5
MLA_SCALE = QW ** -0.5
IDX_SCALE = (IDX_HEADS * IDX_DIM) ** -0.5

C_FQ, C_FG = 0, 3 * BW
C_DQ = C_FG + HEADS
C_IQ = C_DQ + 3 * BW
C_IK = C_IQ + IDX_HEADS * IDX_DIM
C_IW = C_IK + IDX_DIM
C_CQ = C_IW + IDX_HEADS
C_CKV = C_CQ + LORA
C_KPE = C_CKV + LORA
C_SILU = C_KPE + ROPE
C_MERGE = C_SILU + 3 * BW
D_IN = C_MERGE + 3 * D
FOX, DSA, MLA = 0, 1, 2

CW = 512
QCW = 2 * QW
N_IK, N_IW, N_KPE, N_FG = 0, 64, 80, 144
NW = N_FG + HEADS
UNITS = 8
RING = 4
TW = P + SEQ

B_IQ, B_NARROW, B_IQ1, B_DQ, B_DV = 0, 1, 2, 3, 7
B_DG = 9
B_CQ, B_CKV = 17, 18
B_MG0, B_QUP, B_KVUP, B_MG1 = 19, 20, 21, 22
B_FQ, B_FK, B_FV = 29, 31, 33
B_FG = 35
B_OUT = 43
BODIES = 47
U_LAYER = UNITS * BODIES
LOADS_LAYER = U_LAYER // RING
WIDE = [b for b in range(BODIES) if b not in (B_NARROW, B_QUP)]


class Order:

    def __init__(self, events, credit=0):
        self.at = {e: i for i, e in enumerate(events)}
        self.layer, self.credit = len(events), credit
        assert len(self.at) == len(events)

    def after(self, l, event):
        return l * self.layer + (self.at[event] + 1 + self.credit)

    def before(self, l, event):
        return l * self.layer + (self.at[event] + self.credit)


class Links:

    def __init__(self, engine, sem, layer):
        self.engine, self.sem, self.layer, self.n = engine, sem, layer, 0

    def __call__(self, l, ins):
        ins.then_inc(self.sem, 1)
        self.n += 1
        self.engine.wait_ge(self.sem, l * self.layer + self.n)

    def close(self):
        assert self.n == self.layer, (self.n, self.layer)


def head_pairs(branch):
    return [(branch, pair) for pair in range(HEADS // 2)]


def attention_fills(branch, pair):
    return [("scores", branch, pair), ("probs", branch, pair)]


X_FILLS = Order(
    [("x", g) for g in range(4)] + [("iq", 0), ("narrow",), ("cum",), ("iq", 1)]
    + [e for b in range(4) for e in (("index", 2 * b), ("qk", DSA, b), ("index", 2 * b + 1))]
    + [e for p in range(4) for e in attention_fills(DSA, p)]
    + [("code", 0), ("code", 1)] + [("q", j) for j in range(4)] + [("k", j) for j in range(3)]
    + [("scores", MLA, 0), ("k", 3), ("probs", MLA, 0)] + [e for p in range(1, 4) for e in attention_fills(MLA, p)]
    + [("qk", FOX, b) for b in range(4)] + [e for p in range(4) for e in attention_fills(FOX, p)]
    + [("y", g) for g in range(4)])
X_CREDIT = 1
PAIRS = Order(head_pairs(DSA) + head_pairs(MLA) + head_pairs(FOX))


def branch_chunks(branch, bank):
    return [("gate", branch, bank)] + [(m, branch, c) for m in ("merge", "proj") for c in range(bank, 4, 2)]


FREED = [
    Order([("v", DSA, 0)] + branch_chunks(DSA, 0) + [("gate", MLA, 0), ("q", 1), ("q", 3), ("k", 1), ("k", 3)]
          + branch_chunks(MLA, 0)[1:] + [("v", FOX, 0)] + branch_chunks(FOX, 0)[:-2]),
    Order([("v", DSA, 1)] + branch_chunks(DSA, 1) + [("q", 0), ("q", 2), ("k", 0), ("k", 2)]
          + branch_chunks(MLA, 1) + [("v", FOX, 1)] + branch_chunks(FOX, 1)[:-2]),
]
ROWS = [
    Order([("iq", 0), ("iq", 1), ("qk", DSA, 0), ("qk", DSA, 2), ("code", 0), ("q", 0), ("q", 2), ("k", 0),
           ("k", 2), ("qk", FOX, 0), ("qk", FOX, 2)]),
    Order([("narrow",), ("qk", DSA, 1), ("qk", DSA, 3), ("code", 1), ("q", 1), ("q", 3), ("k", 1), ("k", 3),
           ("qk", FOX, 1), ("qk", FOX, 3)]),
]
CHUNKS = 4
NORMS = Order([("x",), ("code", 0), ("code", 1)])
HALVED = Order([("x", g) for g in range(4)] + [("code", 0), ("code", 1)] + [("y", g) for g in range(4)])
TANHS = Order([("gate", b, c) for b in (DSA, MLA, FOX) for c in range(2)])
INDEX_PAIRS = Order([("index", i) for i in range(IDX_HEADS // 2)])
ACT_LINKS, DVE_LINKS = 4, 97


def parity(event):
    return next(i for i in range(2) if event in ROWS[i].at)


def build(nc, x, norm_g, w_wide, w_narrow, w_qup, forget_b, q_norm_g, kv_norm_g, final_norm_g, rope128, rope64, square, negsel, out):
    x_park = nc.dram_tensor("x_park", (P, TT, D), F32).ap()
    with ExitStack() as ctx:
        def sb(name, shape, dt=F32):
            return ctx.enter_context(nc.sbuf_tensor(name, shape, dt))

        def sem(name):
            return ctx.enter_context(nc.semaphore(name))

        raw = sb("raw", [P, RING, 2 * CW])
        w_hi = sb("w_hi", [P, RING, 2 * CW], F32R)
        w_lo = sb("w_lo", [P, RING, 2 * CW], F32R)
        h_hi = sb("h_hi", [P, KT, SEQ], F32R)
        h_lo = sb("h_lo", [P, KT, SEQ], F32R)
        o_hi = sb("o_hi", [P, HEADS, SEQ], F32R)
        o_lo = sb("o_lo", [P, HEADS, SEQ], F32R)
        xy = sb("xy", [P, TT, D])
        qkT = sb("qkT", [P, 2, HEADS, SEQ])
        xs = qkT[:, :, :, :].rearrange("p a h t -> p a (h t)")
        vv = sb("vv", [P, TT, BW])
        gs = sb("gs", [P, TT, BW])
        th = sb("th", [P, TT, D])
        iqT = th[:, 0, :].rearrange("p (b t) -> p b t", b=8)
        ev = sb("ev", [P, TT, CW])
        nat = sb("nat", [P, 2, TT, CW])
        ikT = sb("ikT", [P, SEQ])
        kpT = sb("kpT", [P, SEQ])
        qrT = sb("qrT", [P, HEADS // 2, SEQ])
        score = sb("score", [P, TW])
        dbias = sb("dbias", [P, TW])
        top8 = sb("top8", [P, 2, 8])
        prob = sb("prob", [P, 2, TW])
        probT = sb("probT", [P, 2, TW])
        og = sb("og", [P, 2, TT, HD])
        iw = sb("iw", [P, TT, IDX_HEADS])
        lf = sb("lf", [P, 4, TT, HEADS])
        cumq = sb("cumq", [P, TT, HEADS])
        cumT = sb("cumT", [P, SEQ])
        peak = sb("peak", [P, 2, 2, TT])
        sums = sb("sums", [P, 2, TT])
        rinv = sb("rinv", [P, 2, TT])
        sqp = sb("sqp", [P, TT, CHUNKS])
        ms = sb("ms", [P, 8, TT])
        rp128 = sb("rp128", [P, 2, TT, HD])
        rp64 = sb("rp64", [P, 2, TT, IDX_DIM])
        sq = sb("sq", [P, 3, P])
        mask = sb("mask", [P, TW])
        ones = sb("ones", [P, P])
        nsel = sb("nsel", [HEADS, HEADS, P])
        g_h = sb("g_h", [P, KT])
        g_c = sb("g_c", [P, 2 * LT])
        fb = sb("fb", [P, HEADS])
        fin_g = gs[:, :, :].rearrange("p a n -> p (a n)")
        ident, tri, diag = sq[:, 0, :], sq[:, 1, :], sq[:, 2, :]

        G = ctx.enter_context(nc.psum_tensor("G", [P, 2, TT, CW], F32))
        X = ctx.enter_context(nc.psum_tensor("X", [P, 2, CW], F32))
        PV = ctx.enter_context(nc.psum_tensor("PV", [P, 2, TT, HD], F32))
        OT = ctx.enter_context(nc.psum_tensor("OT", [P, 2, SEQ], F32))
        XT = X[:, :, :].rearrange("p a n -> p (a n)")

        raw_ready = [sem(f"raw_ready{i}") for i in range(RING)]
        hi_ready = sem("hi_ready")
        unit_split = sem("unit_split")
        unit_done = sem("unit_done")
        freed = [sem("freed0"), sem("freed1")]
        rows_ready = [sem("rows_ready0"), sem("rows_ready1")]
        x_done = sem("x_done")
        x_used = sem("x_used")
        xs_ready = sem("xs_ready")
        y_chunk = sem("y_chunk")
        x_chunk = sem("x_chunk")
        hi_taken = sem("hi_taken")
        squared = sem("squared")
        var_ready = sem("var_ready")
        root_ready = sem("root_ready")
        tanh_ready = sem("tanh_ready")
        nope_ready = sem("nope_ready")
        index_used = sem("index_used")
        fabs_ready, flog_ready, logf_ready = sem("fabs_ready"), sem("flog_ready"), sem("logf_ready")
        peak_ready, prob_ready = sem("peak_ready"), sem("prob_ready")
        pv_done, og_ready, ot_done, ot_hi, ot_used = (sem(n) for n in ("pv_done", "og_ready", "ot_done", "ot_hi",
                                                                       "ot_used"))
        x_load = [sem(f"x_load{c}") for c in range(CHUNKS)]
        x_back, x_parked = sem("x_back"), sem("x_parked")
        consts_in, params_in = sem("consts_in"), sem("params_in")
        mask_ready = sem("mask_ready")
        waited = sem("waited")
        act_link, dve_link = sem("act_link"), sem("dve_link")
        fin_in, out_ready, out_stored = sem("fin_in"), sem("out_ready"), sem("out_stored")

        block = ctx.enter_context(nc.Block())

        x_v = x.rearrange("a (t p) d -> p (a t) d", p=P)
        o_v = out.rearrange("a (t p) d -> p (a t) d", p=P)
        TILES = ((0, P), (P, TW))

        @block.sync
        def _(sp):
            def load(l, b, src, width=CW):
                for p in range(UNITS):
                    sp.wait_ge(unit_split, l * U_LAYER + (UNITS * b + p + 1))
                    sp.dma_start(raw[:, p % RING, 0:2 * width], src[p]).then_inc(raw_ready[p % RING], 16)

            def load_wide(l, first, end):
                skipped = first - WIDE.index(first)
                with sp.Fori(first, end) as b:
                    load(l, b, w_wide[l, b - skipped])

            for c in range(CHUNKS):
                sp.dma_start(xy[:, :, c * CW:(c + 1) * CW], x_v[:, :, c * CW:(c + 1) * CW]).then_inc(x_load[c], 16)
            sp.dma_start(rp128[:, :, :, :], rope128).then_inc(consts_in, 16)
            sp.dma_start(rp64[:, :, :, :], rope64).then_inc(consts_in, 16)
            sp.dma_start(sq[:, :, :], square).then_inc(consts_in, 16)
            sp.dma_start(nsel[:, :, :], negsel).then_inc(consts_in, 16)
            with sp.Fori(0, DEPTH) as l:
                sp.wait_ge(y_chunk, CHUNKS * l + 1)
                sp.dma_start(g_h[:, :], norm_g[l]).then_inc(params_in, 16)
                sp.dma_start(g_c[:, 0:LT], q_norm_g[l]).then_inc(params_in, 16)
                sp.dma_start(g_c[:, LT:2 * LT], kv_norm_g[l]).then_inc(params_in, 16)
                sp.dma_start(fb[:, :], forget_b[l].unsqueeze(0).broadcast_to([P, HEADS])).then_inc(params_in, 16)
                load(l, B_IQ, w_wide[l, 0])
                load(l, B_NARROW, w_narrow[l], NW)
                sp.wait_ge(x_chunk, CHUNKS * l + CHUNKS)
                sp.dma_start(x_park, xy[:, :, :]).then_inc(x_parked, 16)
                load_wide(l, B_IQ1, B_QUP)
                load(l, B_QUP, w_qup[l], QCW)
                load_wide(l, B_KVUP, B_OUT + 1)
                sp.wait_ge(x_done, X_FILLS.after(l, ("y", 3)))
                sp.wait_ge(x_parked, 16 * l + 16)
                sp.dma_start(xy[:, :, :], x_park).then_inc(x_back, 16)
                load_wide(l, B_OUT + 1, BODIES)
            sp.wait_ge(x_chunk, CHUNKS * DEPTH + 1)
            sp.dma_start(fin_g, final_norm_g.unsqueeze(0).broadcast_to([P, D])).then_inc(fin_in, 16)
            for c in range(CHUNKS):
                at = slice(c * CW, (c + 1) * CW)
                sp.wait_ge(out_ready, c + 1)
                sp.dma_start(o_v[:, :, at], xy[:, :, at]).then_inc(out_stored, 16)
            sp.wait_ge(out_stored, 16 * CHUNKS)

        @block.tensor
        def _(pe):
            def fill(l, event):
                pe.wait_ge(x_used, X_FILLS.before(l, event) + X_CREDIT)

            def units(l, b, width, plan, hi, lo):
                for p in range(UNITS):
                    ks, bank, start, stop, before = plan(p)
                    if start and before:
                        pe.wait_ge(*before)
                    pe.wait_ge(unit_split, l * U_LAYER + (UNITS * b + p + 1 + RING))
                    for i, k in enumerate(ks):
                        for t in range(TT):
                            dst = G[:, bank, t, 0:width]
                            at = slice(t * P, (t + 1) * P)
                            cols = slice(i * width, (i + 1) * width)
                            wh, wl = w_hi[:, p % RING, cols], w_lo[:, p % RING, cols]
                            pe.matmul(dst, hi[:, k, at], wh, start=start and i == 0, stop=False)
                            pe.matmul(dst, hi[:, k, at], wl, start=False, stop=False)
                            mm = pe.matmul(dst, lo[:, k, at], wh, start=False, stop=stop and i == 1)
                    mm.then_inc(unit_done, 1)
                    yield p

            def out_of(l, bank, *event):
                if event[:2] == ("proj", FOX):
                    return y_chunk, CHUNKS * l + event[2] + 2
                return freed[bank], FREED[bank].after(l, event)

            def w_in_units(l, b, bank, before, width=CW):
                return units(l, b, width, lambda p: ((2 * p, 2 * p + 1), bank, p == 0, p == UNITS - 1, before),
                             h_hi, h_lo)

            def proj_units(l, b, branch, c0):
                def plan(p):
                    c = c0 + p // 4
                    before = out_of(l, c % 2, *(("merge", branch, c + 2) if c < 2 else ("proj", branch, c - 2)))
                    return (2 * (p % 4), 2 * (p % 4) + 1), c % 2, p % 4 == 0, p % 4 == 3, before
                return units(l, b, CW, plan, o_hi, o_lo)

            def up_units(l, b, base, width, before):
                def plan(p):
                    return ((base + 2 * (p % 2), base + 2 * (p % 2) + 1), 1 - p // 2 % 2, p % 2 == 0, p % 2 == 1,
                            before[p // 2])
                return units(l, b, width, plan, o_hi, o_lo)

            def transposes(l, event, blocks):
                i = parity(event)
                pe.wait_ge(rows_ready[i], ROWS[i].after(l, event))
                fill(l, event)
                for j in range(blocks):
                    for t in range(TT):
                        mm = pe.transpose(XT[:, j * SEQ + t * P:j * SEQ + (t + 1) * P],
                                          nat[:, i, t, j * P:(j + 1) * P], ident)
                mm.then_inc(x_done, 1)

            def index_scores(l, pair):
                fill(l, ("index", pair))
                for e in range(2):
                    r = slice(IDX_DIM * e, IDX_DIM * (e + 1))
                    pe.matmul(X[:, e, 0:P], iqT[r, pair, 0:P], ikT[r, 0:P], start=True, stop=True)
                    mm = pe.matmul(X[:, e, P:TW], iqT[r, pair, P:SEQ], ikT[r, :], start=True, stop=True)
                mm.then_inc(x_done, 1)

            def scores(l, branch, pair):
                fill(l, ("scores", branch, pair))
                for e in range(2):
                    h = 2 * pair + e
                    for t, (a, z) in enumerate(TILES):
                        at, keys, dst = slice(t * P, (t + 1) * P), slice(0, (t + 1) * P), X[:, e, a:z]
                        mm = pe.matmul(dst, qkT[:, 0, h, at], qkT[:, 1, h, keys], start=True, stop=branch == DSA)
                        if branch == MLA:
                            r = slice(ROPE * e, ROPE * (e + 1))
                            mm = pe.matmul(dst, qrT[r, pair, at], kpT[r, keys], start=False, stop=True)
                        if branch == FOX:
                            mm = pe.matmul(dst, nsel[:, h, :], cumT[0:HEADS, keys], start=False, stop=True)
                mm.then_inc(x_done, 1)

            def turn_probs(l, branch, pair):
                pe.wait_ge(prob_ready, PAIRS.after(l, (branch, pair)))
                fill(l, ("probs", branch, pair))
                for e in range(2):
                    for j in range(3):
                        mm = pe.transpose(X[:, e, j * P:(j + 1) * P], prob[:, e, j * P:(j + 1) * P], ident)
                mm.then_inc(x_done, 1)

            def values(l, branch, pair):
                pe.wait_ge(x_used, X_FILLS.after(l, ("probs", branch, pair)) + X_CREDIT)
                for e in range(2):
                    h = slice((2 * pair + e) * HD, (2 * pair + e + 1) * HD)
                    pe.matmul(PV[:, e, 0, :], probT[:, e, 0:P], vv[:, 0, h], start=True, stop=True)
                    pe.matmul(PV[:, e, 1, :], probT[:, e, P:2 * P], vv[:, 0, h], start=True, stop=False)
                    mm = pe.matmul(PV[:, e, 1, :], probT[:, e, 2 * P:TW], vv[:, 1, h], start=False, stop=True)
                mm.then_inc(pv_done, 1)

            def turn_heads(l, branch, pair):
                pe.wait_ge(og_ready, PAIRS.after(l, (branch, pair)))
                pe.wait_ge(ot_used, PAIRS.before(l, (branch, pair)) + 1)
                for e in range(2):
                    for t in range(TT):
                        mm = pe.transpose(OT[:, e, t * P:(t + 1) * P], og[:, e, t, :], ident)
                mm.then_inc(ot_done, 1)

            def attend(l, b, branch, first=0):
                for c in range(first, 2):
                    before = ("k", 2) if branch == MLA else ("v", branch, c)
                    for p in w_in_units(l, b, c, out_of(l, c, *before)):
                        if branch == MLA and p == 0:
                            transposes(l, ("k", 2), 2)
                        if branch == MLA and p == 3:
                            transposes(l, ("k", 3), 2)
                        if c == 1 and p == 1:
                            scores(l, branch, 0)
                        if c == 1 and p == 5:
                            turn_probs(l, branch, 0)
                    b += 1
                for c in range(4):
                    before = ("merge", branch, c - 2) if c > 1 else ("gate", branch, c)
                    if branch == MLA and c == 0:
                        before = ("k", 3)
                    for p in w_in_units(l, b, c % 2, out_of(l, c % 2, *before)):
                        if p == 0:
                            values(l, branch, c)
                        if p == 1 and c < 3:
                            scores(l, branch, c + 1)
                        if p == 3:
                            turn_heads(l, branch, c)
                        if p == 5 and c < 3:
                            turn_probs(l, branch, c + 1)
                    b += 1
                pe.wait_ge(ot_used, PAIRS.after(l, (branch, 3)) + 1)
                for c in (0, 2):
                    for p in proj_units(l, b + c // 2, branch, c):
                        if branch == FOX and c and p in (1, 4, 7):
                            turn_four(l, "y", p // 3)

            def turn_four(l, name, g):
                if name == "x":
                    src = xs
                    pe.wait_ge(xs_ready, CHUNKS * l + (g + 1))
                else:
                    src = xy
                    pe.wait_ge(y_chunk, CHUNKS * l + (g + 2))
                fill(l, (name, g))
                for j in range(4):
                    for t in range(TT):
                        k = 4 * g + j
                        mm = pe.transpose(XT[:, j * SEQ + t * P:j * SEQ + (t + 1) * P],
                                          src[:, t, k * P:(k + 1) * P], ident)
                mm.then_inc(x_done, 1)

            def halves(l, name):
                pe.wait_ge(x_used, X_FILLS.after(l, (name, 3)) + X_CREDIT)

            pe.sem_inc(unit_done, RING)
            pe.wait_ge(consts_in, 64)
            with pe.Fori(0, DEPTH) as l:
                turn_four(l, "x", 0)
                turn_four(l, "x", 1)
                for p in w_in_units(l, B_IQ, 1, None):
                    if p == 1 or p == 3:
                        turn_four(l, "x", p // 2 + 2)
                    if p == 5:
                        halves(l, "x")
                for p in w_in_units(l, B_NARROW, 0, None, NW):
                    pass
                transposes(l, ("iq", 0), 4)
                for p in w_in_units(l, B_IQ1, 1, None):
                    if p == 3:
                        transposes(l, ("narrow",), 2)
                    if p == 6:
                        pe.wait_ge(logf_ready, l + 1)
                        fill(l, ("cum",))
                        pe.matmul(X[:, 0, 0:HEADS], tri, lf[:, 3, 0, :], start=True, stop=True)
                        pe.matmul(X[:, 0, HEADS:2 * HEADS], ones[:, :], lf[:, 3, 0, :], start=True, stop=False)
                        pe.matmul(X[:, 0, HEADS:2 * HEADS], tri, lf[:, 3, 1, :], start=False, stop=True)
                        pe.matmul(X[0:HEADS, 1, 0:P], lf[:, 3, 0, :], tri, start=True, stop=True)
                        pe.matmul(X[0:HEADS, 1, P:SEQ], lf[:, 3, 0, :], ones[:, :], start=True, stop=False)
                        mm = pe.matmul(X[0:HEADS, 1, P:SEQ], lf[:, 3, 1, :], tri, start=False, stop=True)
                        mm.then_inc(x_done, 1)
                for b in range(B_DQ, B_DG):
                    n = b - B_DQ - 1
                    for p in w_in_units(l, b, (b - B_DQ) % 2, None):
                        if n >= 0 and n < 4 and p == 0:
                            index_scores(l, 2 * n)
                        if n < 4 and p == 3:
                            transposes(l, ("qk", DSA, n) if n >= 0 else ("iq", 1), 4)
                        if n >= 0 and n < 4 and p == 5:
                            index_scores(l, 2 * n + 1)
                attend(l, B_DG, DSA)
                for p in w_in_units(l, B_CQ, 0, out_of(l, 0, "proj", DSA, 2)):
                    pass
                for i, (b, before) in enumerate(((B_CKV, out_of(l, 1, "proj", DSA, 3)), (B_MG0, None))):
                    for p in w_in_units(l, b, 1 - i, before):
                        if p == 5:
                            transposes(l, ("code", i), 4)
                pe.wait_ge(x_used, X_FILLS.after(l, ("code", 1)) + X_CREDIT)
                for p in up_units(l, B_QUP, 0, QCW, (None, out_of(l, 0, "gate", MLA, 0), out_of(l, 1, "q", 0),
                                                       out_of(l, 0, "q", 1))):
                    if p == 4 or p == 6:
                        transposes(l, ("q", p // 2 - 2), 3)
                for p in up_units(l, B_KVUP, LT, CW, (out_of(l, 1, "q", 2), out_of(l, 0, "q", 3), out_of(l, 1, "k", 0),
                                                       out_of(l, 0, "k", 1))):
                    if p == 0 or p == 2:
                        transposes(l, ("q", p // 2 + 2), 3)
                    if p == 4 or p == 6:
                        transposes(l, ("k", p // 2 - 2), 2)
                attend(l, B_MG1, MLA, first=1)
                for b in range(B_FQ, B_FG):
                    n = b - B_FQ - 1
                    before = out_of(l, n + 1, "proj", MLA, n + 3) if n < 1 else None
                    for p in w_in_units(l, b, (b - B_FQ) % 2, before):
                        if 0 <= n < 4 and p == 3:
                            transposes(l, ("qk", FOX, n), 4)
                attend(l, B_FG, FOX)
                for c in range(CHUNKS):
                    before = (x_chunk, CHUNKS * l + (CHUNKS + c - 1)) if c > 1 else out_of(l, c, "proj", FOX, 2 + c)
                    for p in w_in_units(l, B_OUT + c, c % 2, before):
                        if c == 0 and p == 3:
                            turn_four(l, "y", 3)
                        if c == 0 and p == 5:
                            halves(l, "y")

        @block.scalar
        def _(act):
            link = Links(act, act_link, ACT_LINKS)

            def units(l, b, width=CW):
                for p in range(UNITS):
                    act.wait_ge(raw_ready[p % RING], l * (16 * LOADS_LAYER) + 16 * (2 * b + p // RING + 1))
                    act.wait_ge(unit_done, l * U_LAYER + (UNITS * b + p + 1))
                    act.copy(w_hi[:, p % RING, 0:2 * width], raw[:, p % RING, 0:2 * width]).then_inc(hi_ready, 1)
                    yield p

            def chunk_in(l, b, p=UNITS - 1):
                act.wait_ge(unit_done, l * U_LAYER + (UNITS * b + p + 1 + RING))

            def filled(l, event):
                act.wait_ge(x_done, X_FILLS.after(l, event))

            def gate(l, b, branch, c):
                chunk_in(l, b)
                if c:
                    act.wait_ge(freed[0], FREED[0].after(l, ("gate", branch, 0)))
                act.activation(ev[:, :, :], G[:, c, :, :], ACT.Tanh, scale=0.5).then_inc(tanh_ready, 1)

            def merge(l, b, c):
                chunk_in(l, b)
                act.activation(th[:, :, c * CW:(c + 1) * CW], G[:, c % 2, :, :], ACT.Tanh, scale=0.5)\
                   .then_inc(freed[c % 2], 1)

            def softmax(l, branch, pair):
                scale = MLA_SCALE if branch == MLA else SCALE
                act.wait_ge(peak_ready, PAIRS.after(l, (branch, pair)))
                for e in range(2):
                    for t, (a, z) in enumerate(TILES):
                        last = act.activation(prob[:, e, a:z], prob[:, e, a:z], ACT.Exp, scale=scale,
                                              bias=peak[:, 1, e, t:t + 1], accum_out=sums[:, e, t:t + 1])
                last.then_inc(prob_ready, 1)

            def take_probs(l, branch, pair):
                filled(l, ("probs", branch, pair))
                act.copy(probT[:, :, :], X[:, :, 0:TW]).then_inc(x_used, 1)

            def take_heads(l, branch, pair):
                act.wait_ge(ot_done, PAIRS.after(l, (branch, pair)))
                act.copy(o_hi[:, 2 * pair:2 * pair + 2, :], OT[:, :, :]).then_inc(ot_hi, 1)

            def take_values(l, b, bank):
                chunk_in(l, b)
                act.copy(vv[:, :, bank * CW:(bank + 1) * CW], G[:, bank, :, :]).then_inc(freed[bank], 1)

            def latent_kv(l, b, j):
                chunk_in(l, b, 2 * j + 1)
                src = G[:, 1 - j % 2, :, :].rearrange("p t (e c d) -> p t e c d", e=2, c=2)
                for t in range(TT):
                    last = act.copy(nat[:, j % 2, t, 0:2 * HD].rearrange("p (e d) -> p e d", e=2), src[:, t, :, 0, :])
                last.then_inc(rows_ready[j % 2], 1)
                for t in range(TT):
                    last = act.copy(vv[:, t, 2 * j * HD:2 * (j + 1) * HD].rearrange("p (e d) -> p e d", e=2),
                                    src[:, t, :, 1, :])
                last.then_inc(freed[1 - j % 2], 1)

            def take_keys(l, j):
                filled(l, ("k", j))
                act.copy(qkT[:, 1, 2 * j:2 * j + 2, :], X[:, 0, :].rearrange("p (e t) -> p e t", e=2))\
                   .then_inc(x_used, 1)

            def latent_q(l, b, j):
                chunk_in(l, b, 2 * j + 1)
                for t in range(TT):
                    last = act.copy(nat[:, j % 2, t, 0:2 * HD].rearrange("p (e d) -> p e d", e=2),
                                    G[:, 1 - j % 2, t, 0:QCW].rearrange("p (e d) -> p e d", e=2)[:, :, 0:HD])
                last.then_inc(nope_ready, 1)

            def take_queries(l, j):
                filled(l, ("q", j))
                act.copy(qkT[:, 0, 2 * j:2 * j + 2, :], X[:, 0, :].rearrange("p (e t) -> p e t", e=2))
                act.copy(qrT[:, j, :], X[:, 1, 0:SEQ]).then_inc(x_used, 1)

            def take_four(l, event, dst):
                filled(l, event)
                act.copy(dst, X[:, :, :].rearrange("p a (h t) -> p (a h) t", h=2)).then_inc(x_used, 1)

            def attend(l, b, branch, first=0):
                for c in range(first, 2):
                    for p in units(l, b):
                        if branch != MLA and p == 1:
                            if c == 0:
                                take_values(l, b - 1, 1)
                            else:
                                gate(l, b - 1, branch, 0)
                        if branch == MLA and p == 1:
                            take_keys(l, 2)
                            latent_kv(l, b - 1, 3)
                        if c == 1 and p == 4:
                            softmax(l, branch, 0)
                        if branch == MLA and p == 5:
                            take_keys(l, 3)
                        if c == 1 and p == 7:
                            take_probs(l, branch, 0)
                    b += 1
                for c in range(4):
                    for p in units(l, b):
                        if p == 1:
                            if c == 0:
                                gate(l, b - 1, branch, 1)
                            else:
                                merge(l, b - 1, c - 1)
                        if p == 4 and c < 3:
                            softmax(l, branch, c + 1)
                        if p == 5:
                            take_heads(l, branch, c)
                        if p == 7 and c < 3:
                            take_probs(l, branch, c + 1)
                    b += 1
                for c in range(2):
                    for p in units(l, b + c):
                        if c == 0 and p == 1:
                            merge(l, b - 1, 3)
                        if branch == FOX and c == 1 and (p == 3 or p == 6):
                            take_y(l, p // 3 - 1)

            def root(l, event):
                act.wait_ge(var_ready, NORMS.after(l, event))
                link(l, act.activation(ms[:, 2, :], ms[:, 1, :], ACT.Ln))
                act.activation(ms[:, 3, :], ms[:, 2, :], ACT.Exp, scale=-0.5).then_inc(root_ready, 1)

            def take_upper(l, event, hi, g=None):
                filled(l, event)
                if g is None:
                    last = act.copy(hi, X[:, :, :].rearrange("p a (h t) -> p (a h) t", h=2))
                else:
                    for j in range(4):
                        last = act.activation(hi[:, j, :], XT[:, j * SEQ:(j + 1) * SEQ], ACT.Copy,
                                              scale=g[:, j:j + 1])
                last.then_inc(hi_taken, 1)

            def take_x(l, g):
                take_upper(l, ("x", g), h_hi[:, 4 * g:4 * g + 4, :], g_h[:, 4 * g:4 * g + 4])

            def take_y(l, g):
                take_upper(l, ("y", g), h_hi[:, 4 * g:4 * g + 4, :])

            def squares(l, c):
                act.wait_ge(x_chunk, CHUNKS * l + (c + 1))
                for t in range(TT):
                    last = act.activation(th[:, t, c * CW:(c + 1) * CW], xy[:, t, c * CW:(c + 1) * CW], ACT.Square,
                                          accum_out=sqp[:, t, c:c + 1])
                if c == CHUNKS - 1:
                    last.then_inc(squared, 1)

            for c in range(CHUNKS - 1):
                squares(0, c)
            with act.Fori(0, DEPTH) as l:
                squares(l, CHUNKS - 1)
                for p in units(l, B_IQ):
                    if p == 0:
                        root(l, ("x",))
                        act.wait_ge(params_in, 64 * l + 64)
                    if p == 2:
                        take_x(l, 0)
                    if p == 3:
                        take_x(l, 1)
                    if p == 5 or p == 7:
                        take_x(l, p // 2)
                for p in units(l, B_NARROW, NW):
                    pass
                for p in units(l, B_IQ1):
                    if p == 1:
                        take_four(l, ("iq", 0), iqT[:, 0:4, :])
                    if p == 3:
                        act.wait_ge(fabs_ready, l + 1)
                        link(l, act.activation(lf[:, 2, :, :], lf[:, 1, :, :], ACT.Exp, scale=-1.0))
                        act.activation(lf[:, 2, :, :], lf[:, 2, :, :], ACT.Ln, bias=1.0).then_inc(flog_ready, 1)
                    if p == 5:
                        filled(l, ("narrow",))
                        act.copy(ikT[:, :], X[:, 0, 0:SEQ])
                        act.copy(kpT[:, :], X[:, 0, SEQ:2 * SEQ]).then_inc(x_used, 1)
                for b in range(B_DQ, B_DG):
                    n = b - B_DQ - 1
                    for p in units(l, b):
                        if b == B_DV + 1 and p == 1:
                            take_values(l, b - 1, 0)
                        if 0 <= n < 4 and (p == 2 or p == 7):
                            pair = 2 * n + (p == 7)
                            filled(l, ("index", pair))
                            act.wait_ge(index_used, INDEX_PAIRS.before(l, ("index", pair)) + 1)
                            act.activation(prob[:, :, :], X[:, :, 0:TW], ACT.Relu).then_inc(x_used, 1)
                        if n < 4 and p == 5:
                            if n < 0:
                                take_four(l, ("iq", 1), iqT[:, 4:8, :])
                            else:
                                take_four(l, ("qk", DSA, n), qkT[:, n // 2, 4 * (n % 2):4 * (n % 2) + 4, :])
                attend(l, B_DG, DSA)
                for p in units(l, B_CQ):
                    pass
                for i, b in enumerate((B_CKV, B_MG0)):
                    for p in units(l, b):
                        if p == 1:
                            chunk_in(l, b - 1)
                            for t in range(TT):
                                last = act.activation((prob, probT)[t][:, :, 0:CW // 2],
                                                      G[:, i, t, :].rearrange("p (a n) -> p a n", a=2), ACT.Square,
                                                      accum_out=ms[:, 0, t:t + 1])
                            last.then_inc(squared, 1)
                        if p == 3:
                            root(l, ("code", i))
                        if p == 7:
                            take_upper(l, ("code", i), o_hi[:, LT * i:LT * (i + 1), :], g_c[:, LT * i:LT * (i + 1)])
                for p in units(l, B_QUP, QCW):
                    if p == 1:
                        gate(l, B_MG0, MLA, 0)
                    if p in (3, 5, 7):
                        latent_q(l, B_QUP, (p - 3) // 2)
                    if p == 6:
                        take_queries(l, 0)
                for p in units(l, B_KVUP):
                    if p == 0 or p == 2 or p == 4:
                        take_queries(l, 1 + p // 2)
                    if p == 1:
                        latent_q(l, B_QUP, 3)
                    if p == 3 or p == 5:
                        latent_kv(l, B_KVUP, (p - 3) // 2)
                    if p == 6:
                        take_keys(l, 0)
                    if p == 7:
                        latent_kv(l, B_KVUP, 2)
                        take_keys(l, 1)
                attend(l, B_MG1, MLA, first=1)
                for b in range(B_FQ, B_FG):
                    n = b - B_FQ - 1
                    for p in units(l, b):
                        if 0 <= n < 4 and p == 1:
                            chunk_in(l, b - 1)
                            act.copy(nat[:, n % 2, :, :], G[:, n % 2, :, :]).then_inc(rows_ready[n % 2], 1)
                        if n == 4 and p == 1:
                            take_values(l, b - 1, 0)
                        if 0 <= n < 4 and p == 5:
                            take_four(l, ("qk", FOX, n), qkT[:, n // 2, 4 * (n % 2):4 * (n % 2) + 4, :])
                attend(l, B_FG, FOX)
                for c in range(CHUNKS):
                    for p in units(l, B_OUT + c):
                        if c == 0 and (p == 2 or p == 5):
                            take_y(l, 2 + p // 5)
                        if c and p == 3:
                            squares(l + 1, c - 1)
                link.close()
            squares(DEPTH, CHUNKS - 1)
            act.wait_ge(var_ready, NORMS.layer * DEPTH + 1)
            act.activation(ms[:, 2, :], ms[:, 1, :], ACT.Ln).then_inc(act_link, 1)
            act.wait_ge(act_link, ACT_LINKS * DEPTH + 1)
            act.activation(ms[:, 3, :], ms[:, 2, :], ACT.Exp, scale=-0.5).then_inc(root_ready, 1)

        @block.vector
        def _(dve):
            link = Links(dve, dve_link, DVE_LINKS)

            def units(l, b, width=CW):
                for p in range(UNITS):
                    dve.wait_ge(hi_ready, l * U_LAYER + (UNITS * b + p + 1))
                    r = p % RING
                    dve.tensor_tensor(w_lo[:, r, 0:2 * width], raw[:, r, 0:2 * width],
                                      w_hi[:, r, 0:2 * width].bitcast(F32), ALU.subtract).then_inc(unit_split, 1)
                    yield p

            def chunk_in(l, b, p=UNITS - 1):
                dve.wait_ge(unit_done, l * U_LAYER + (UNITS * b + p + 1 + RING))

            def filled(l, event):
                dve.wait_ge(x_done, X_FILLS.after(l, event))

            def rotate(l, t1, src, dst, table, heads, dim):
                half = dim // 2
                for t in range(TT):
                    cos = table[:, 0, t, :].unsqueeze(1).broadcast_to([P, heads, dim])
                    dve.tensor_tensor(t1[:, t], src[:, t], cos, ALU.mult)
                    sin = table[:, 1, t, :].unsqueeze(1).broadcast_to([P, heads, dim])
                    dve.tensor_tensor(dst[:, t, :, 0:half], src[:, t, :, half:dim], sin[:, :, 0:half], ALU.mult)
                    last = dve.tensor_tensor(dst[:, t, :, half:dim], src[:, t, :, 0:half], sin[:, :, half:dim],
                                             ALU.mult)
                return last

            def rotate_chunk(l, b, bank, i, table, heads, dim):
                chunk_in(l, b)
                src = G[:, bank, :, :].rearrange("p t (h d) -> p t h d", h=heads)
                t1 = ev[:, :, :].rearrange("p t (h d) -> p t h d", h=heads)
                dst = nat[:, i, :, :].rearrange("p t (h d) -> p t h d", h=heads)
                link(l, rotate(l, t1, src, dst, table, heads, dim))
                dve.tensor_tensor(nat[:, i, :, :], nat[:, i, :, :], ev[:, :, :], ALU.add).then_inc(rows_ready[i], 1)

            def norm_factor(l, event, width):
                dve.wait_ge(squared, NORMS.after(l, event))
                if event == ("x",):
                    link(l, dve.tensor_reduce(ms[:, 0, :], sqp[:, :, :], AX_X, ALU.add))
                dve.tensor_scalar(ms[:, 1, :], ms[:, 0, :], 1.0 / width, EPS, ALU.mult, ALU.add)\
                   .then_inc(var_ready, 1)

            def newton(l, event):
                dve.wait_ge(root_ready, NORMS.after(l, event))
                link(l, dve.tensor_tensor(ms[:, 4, :], ms[:, 3, :], ms[:, 3, :], ALU.mult))
                link(l, dve.tensor_tensor(ms[:, 5, :], ms[:, 4, :], ms[:, 1, :], ALU.mult))
                link(l, dve.tensor_scalar(ms[:, 6, :], ms[:, 5, :], -0.5, 1.5, ALU.mult, ALU.add))
                link(l, dve.tensor_tensor(ms[:, 7, :], ms[:, 3, :], ms[:, 6, :], ALU.mult))

            def take_lower(l, event, hi, lo, g=None):
                dve.wait_ge(hi_taken, HALVED.after(l, event))
                filled(l, event)
                if g is None:
                    last = dve.tensor_tensor(lo, X[:, :, :].rearrange("p a (h t) -> p (a h) t", h=2),
                                             hi.bitcast(F32), ALU.subtract)
                else:
                    for j in range(4):
                        last = dve.scalar_tensor_tensor(out=lo[:, j, :], in0=XT[:, j * SEQ:(j + 1) * SEQ],
                                                        scalar=g[:, j:j + 1], in1=hi[:, j, :].bitcast(F32),
                                                        op0=ALU.mult, op1=ALU.subtract)
                last.then_inc(x_used, 1)

            def gate(l, branch, c):
                dve.wait_ge(tanh_ready, TANHS.after(l, ("gate", branch, c)))
                dve.scalar_tensor_tensor(out=gs[:, :, c * CW:(c + 1) * CW], in0=ev[:, :, :], scalar=1.0,
                                         in1=G[:, c, :, :], op0=ALU.add, op1=ALU.mult).then_inc(freed[c], 1)

            def logits(l, branch, pair):
                filled(l, ("scores", branch, pair))
                if branch == FOX:
                    for e in range(2):
                        for t, (a, z) in enumerate(TILES):
                            h = 2 * pair + e
                            last = dve.scalar_tensor_tensor(out=prob[:, e, a:z], in0=X[:, e, a:z],
                                                            scalar=cumq[:, t, h:h + 1], in1=mask[:, a:z],
                                                            op0=ALU.add, op1=ALU.add)
                else:
                    bias = dbias if branch == DSA else mask
                    last = dve.tensor_tensor(prob[:, :, :], X[:, :, 0:TW],
                                             bias[:, :].unsqueeze(1).broadcast_to([P, 2, TW]), ALU.add)
                last.then_inc(x_used, 1)
                dve.wait_ge(x_used, X_FILLS.after(l, ("scores", branch, pair)) + X_CREDIT)
                for t, (a, z) in enumerate(TILES):
                    last = dve.tensor_reduce(peak[:, 0, :, t], prob[:, :, a:z], AX_X, ALU.max)
                link(l, last)
                scale = MLA_SCALE if branch == MLA else SCALE
                dve.tensor_scalar(peak[:, 1, :, :], peak[:, 0, :, :], -scale, None, ALU.mult).then_inc(peak_ready, 1)

            def gate_heads(l, branch, pair):
                dve.wait_ge(prob_ready, PAIRS.after(l, (branch, pair)))
                link(l, dve.reciprocal(rinv[:, :, :], sums[:, :, :]))
                link(l, dve.tensor_scalar(rinv[:, :, :], rinv[:, :, :], 0.5, None, ALU.mult))
                dve.wait_ge(pv_done, PAIRS.after(l, (branch, pair)))
                for e in range(2):
                    h = slice((2 * pair + e) * HD, (2 * pair + e + 1) * HD)
                    for t in range(TT):
                        last = dve.scalar_tensor_tensor(out=og[:, e, t, :], in0=PV[:, e, t, :],
                                                        scalar=rinv[:, e, t:t + 1], in1=gs[:, t, h],
                                                        op0=ALU.mult, op1=ALU.mult)
                last.then_inc(og_ready, 1)

            def rest_of_heads(l, branch, pair):
                dve.wait_ge(ot_hi, PAIRS.after(l, (branch, pair)))
                at = slice(2 * pair, 2 * pair + 2)
                dve.tensor_tensor(o_lo[:, at, :], OT[:, :, :], o_hi[:, at, :].bitcast(F32), ALU.subtract)\
                   .then_inc(ot_used, 1)

            def project(l, b, branch, c):
                chunk_in(l, b, 4 * (c % 2) + 3)
                if branch == DSA and c == 0:
                    dve.wait_ge(x_parked, 16 * l + 16)
                at = slice(c * CW, (c + 1) * CW)
                link(l, dve.scalar_tensor_tensor(out=ev[:, :, :], in0=th[:, :, at], scalar=1.0, in1=G[:, c % 2, :, :],
                                                 op0=ALU.add, op1=ALU.mult))
                if branch == DSA:
                    last = dve.tensor_scalar(xy[:, :, at], ev[:, :, :], 0.5, None, ALU.mult)
                else:
                    last = dve.scalar_tensor_tensor(out=xy[:, :, at], in0=ev[:, :, :], scalar=0.5, in1=xy[:, :, at],
                                                    op0=ALU.mult, op1=ALU.add)
                last.then_inc(y_chunk if branch == FOX else freed[c % 2], 1)

            def rest_of_x(l, g):
                at = slice(4 * g, 4 * g + 4)
                take_lower(l, ("x", g), h_hi[:, at, :], h_lo[:, at, :], g_h[:, at])

            def rest_of_y(l, g):
                at = slice(4 * g, 4 * g + 4)
                take_lower(l, ("y", g), h_hi[:, at, :], h_lo[:, at, :])

            def add_out(l, c):
                chunk_in(l, B_OUT + c)
                at = slice(c * CW, (c + 1) * CW)
                dve.tensor_tensor(xy[:, :, at], G[:, c % 2, :, :], xy[:, :, at], ALU.add).then_inc(x_chunk, 1)

            def scale_x(l, g):
                at = slice(g * CW, (g + 1) * CW)
                for t in range(TT):
                    last = dve.tensor_scalar(xs[:, t, at], xy[:, t, at], ms[:, 7, t:t + 1], None, ALU.mult)
                last.then_inc(xs_ready, 1)

            def attend(l, b, branch, first=0):
                for c in range(first, 2):
                    for p in units(l, b):
                        if branch == DSA and c == 0 and p == 2:
                            link(l, dve.tensor_scalar(dbias[:, :], score[:, :], TAKEN / 1.5, NEG, ALU.is_gt, ALU.mult))
                            link(l, dve.tensor_tensor(dbias[:, :], dbias[:, :], mask[:, :], ALU.add))
                        if branch != MLA and c == 1 and p == 1:
                            gate(l, branch, 0)
                        if c == 1 and p == 3:
                            logits(l, branch, 0)
                    b += 1
                for c in range(4):
                    for p in units(l, b):
                        if c == 0 and p == 1:
                            gate(l, branch, 1)
                        if p == 2:
                            gate_heads(l, branch, c)
                        if p == 3 and c < 3:
                            logits(l, branch, c + 1)
                        if p == 5:
                            rest_of_heads(l, branch, c)
                    b += 1
                for c in range(2):
                    for p in units(l, b + c):
                        if c == 1 and p == 1:
                            project(l, b, branch, 1)
                        if branch == FOX and c == 1 and p == 3:
                            rest_of_y(l, 0)
                        if p == 5:
                            project(l, b + c, branch, 2 * c)
                        if branch == FOX and c == 1 and p == 6:
                            rest_of_y(l, 1)

            def latent_q(l, b, j):
                dve.wait_ge(nope_ready, l * 4 + (j + 1))
                chunk_in(l, b, 2 * j + 1)
                src = G[:, 1 - j % 2, :, 0:QCW].rearrange("p t (e d) -> p t e d", e=2)[:, :, :, HD:QW]
                dst = nat[:, j % 2, :, 2 * HD:3 * HD].rearrange("p t (e d) -> p t e d", e=2)
                t1 = ev[:, :, 0:HD].rearrange("p t (e d) -> p t e d", e=2)
                if j:
                    dve.wait_ge(rows_ready[(j - 1) % 2], ROWS[(j - 1) % 2].after(l, ("q", j - 1)))
                else:
                    dve.wait_ge(freed[0], FREED[0].after(l, ("gate", MLA, 0)))
                rotate(l, t1, src, dst, rp64, 2, ROPE).then_inc(freed[1 - j % 2], 1)
                dve.wait_ge(freed[1 - j % 2], FREED[1 - j % 2].after(l, ("q", j)))
                dve.tensor_tensor(nat[:, j % 2, :, 2 * HD:3 * HD], nat[:, j % 2, :, 2 * HD:3 * HD], ev[:, :, 0:HD],
                                  ALU.add).then_inc(rows_ready[j % 2], 1)

            dve.sem_inc(unit_split, RING)
            dve.sem_inc(x_used, X_CREDIT)
            for free in (ot_used, index_used, y_chunk):
                dve.sem_inc(free, 1)
            dve.memset(ones[:, :], 1.0)
            dve.memset(ms[:, :, :], 1.0)
            dve.wait_ge(consts_in, 64)
            dve.tensor_scalar(mask[:, 0:P], diag, 1.0, None, ALU.mult)
            dve.tensor_scalar(mask[:, P:2 * P], diag, 0.0, None, ALU.mult)
            dve.tensor_scalar(mask[:, 2 * P:TW], diag, 1.0, None, ALU.mult).then_inc(mask_ready, 1)
            dve.wait_ge(mask_ready, 1)
            for c in range(CHUNKS):
                dve.wait_ge(x_load[c], 16)
                dve.sem_inc(x_chunk, 1)
            with dve.Fori(0, DEPTH) as l:
                norm_factor(l, ("x",), D)
                for p in units(l, B_IQ):
                    if p == 0:
                        newton(l, ("x",))
                        dve.wait_ge(params_in, 64 * l + 64)
                        scale_x(l, 0)
                        scale_x(l, 1)
                    if p == 2:
                        rest_of_x(l, 0)
                    if p == 3:
                        scale_x(l, 2)
                        scale_x(l, 3)
                        rest_of_x(l, 1)
                    if p == 5 or p == 7:
                        rest_of_x(l, p // 2)
                for p in units(l, B_NARROW, NW):
                    if p == 1:
                        rotate_chunk(l, B_IQ, 1, 0, rp64, 8, IDX_DIM)
                for p in units(l, B_IQ1):
                    if p == 1:
                        chunk_in(l, B_NARROW)
                        z = G[:, 0, :, :]
                        dve.tensor_scalar(iw[:, :, :], z[:, :, N_IW:N_KPE], IDX_SCALE, None, ALU.mult)
                        link(l, dve.tensor_tensor(lf[:, 0, :, :], z[:, :, N_FG:NW],
                                                  fb[:, :].unsqueeze(1).broadcast_to([P, TT, HEADS]), ALU.add))
                        src = z[:, :, 0:2 * N_KPE].rearrange("p t (e d) -> p t e d", e=2)[:, :, :, 0:ROPE]
                        dup = nat[:, 1, :, 0:2 * P].rearrange("p t (e c d) -> p t e c d", e=2, c=2)
                        t1 = ev[:, :, 0:P].rearrange("p t (e d) -> p t e d", e=2)
                        link(l, rotate(l, t1, src, dup[:, :, :, 0, :], rp64, 2, ROPE))
                        for t in range(TT):
                            dve.tensor_tensor(dup[:, t, :, 1, :], dup[:, t, :, 0, :], t1[:, t], ALU.add)
                        for t in range(TT):
                            last = dve.tensor_tensor(dup[:, t, :, 0, :], dup[:, t, :, 0, :], t1[:, t], ALU.add)
                        last.then_inc(rows_ready[1], 1)
                    if p == 2:
                        link(l, dve.tensor_scalar(lf[:, 1, :, :], lf[:, 0, :, :], -1.0, None, ALU.mult))
                        dve.tensor_tensor(lf[:, 1, :, :], lf[:, 1, :, :], lf[:, 0, :, :], ALU.max)\
                           .then_inc(fabs_ready, 1)
                    if p == 4:
                        dve.wait_ge(flog_ready, l + 1)
                        dve.scalar_tensor_tensor(out=lf[:, 3, :, :], in0=lf[:, 0, :, :], scalar=0.0,
                                                 in1=lf[:, 2, :, :], op0=ALU.min, op1=ALU.subtract)\
                           .then_inc(logf_ready, 1)
                    if p == 7:
                        filled(l, ("cum",))
                        dve.tensor_scalar(cumq[:, :, :], X[:, 0, 0:2 * HEADS].rearrange("p (t h) -> p t h", t=TT),
                                          1 / SCALE, None, ALU.mult)
                        dve.tensor_scalar(cumT[0:HEADS, :], X[0:HEADS, 1, 0:SEQ], 1 / SCALE, None, ALU.mult)\
                           .then_inc(x_used, 1)
                for b in range(B_DQ, B_DG):
                    n = b - B_DQ - 1
                    for p in units(l, b):
                        if b == B_DV + 1:
                            if p == 0:
                                link(l, dve.tensor_tensor(score[:, :], score[:, :], mask[:, :], ALU.add))
                            dve.sem_inc(waited, 1)
                            for t, (a, z) in enumerate(TILES):
                                last = dve.max(top8[:, t, :], score[:, a:z])
                            link(l, last)
                            dve.sem_inc(waited, 1)
                            for t, (a, z) in enumerate(TILES):
                                last = dve.match_replace(score[:, a:z], top8[:, t, :], score[:, a:z], TAKEN)
                            link(l, last)
                        if n < 0 and p == 1:
                            rotate_chunk(l, b - 1, 1, 0, rp64, 8, IDX_DIM)
                        if 0 <= n < 4 and p == 1:
                            rotate_chunk(l, b - 1, n % 2, n % 2, rp128, 4, HD)
                        if 0 <= n < 4 and (p == 2 or p == 7):
                            pair = 2 * n + (p == 7)
                            dve.wait_ge(x_used, X_FILLS.after(l, ("index", pair)) + X_CREDIT)
                            for e in range(2):
                                for t, (a, z) in enumerate(TILES):
                                    w = iw[:, t, 2 * pair + e:2 * pair + e + 1]
                                    if pair == 0 and e == 0:
                                        last = dve.tensor_scalar(score[:, a:z], prob[:, e, a:z], w, None, ALU.mult)
                                    else:
                                        last = dve.scalar_tensor_tensor(out=score[:, a:z], in0=prob[:, e, a:z],
                                                                        scalar=w, in1=score[:, a:z], op0=ALU.mult,
                                                                        op1=ALU.add)
                                if e == 0:
                                    link(l, last)
                            last.then_inc(index_used, 1)
                            dve.wait_ge(index_used, INDEX_PAIRS.after(l, ("index", pair)) + 1)
                attend(l, B_DG, DSA)
                for p in units(l, B_CQ):
                    if p == 1:
                        project(l, B_CQ - 1, DSA, 3)
                for i, b in enumerate((B_CKV, B_MG0)):
                    for p in units(l, b):
                        if p == 2:
                            norm_factor(l, ("code", i), LORA)
                        if p == 4:
                            newton(l, ("code", i))
                            for t in range(TT):
                                last = dve.tensor_scalar(nat[:, i, t, :], G[:, i, t, :], ms[:, 7, t:t + 1], None,
                                                         ALU.mult)
                            last.then_inc(rows_ready[i], 1)
                        if p == 7:
                            at = slice(LT * i, LT * (i + 1))
                            take_lower(l, ("code", i), o_hi[:, at, :], o_lo[:, at, :], g_c[:, at])
                for p in units(l, B_QUP, QCW):
                    if p == 1:
                        gate(l, MLA, 0)
                    if p in (3, 5, 7):
                        latent_q(l, B_QUP, (p - 3) // 2)
                for p in units(l, B_KVUP):
                    if p == 1:
                        latent_q(l, B_QUP, 3)
                attend(l, B_MG1, MLA, first=1)
                for b in range(B_FQ, B_FG):
                    for p in units(l, b):
                        if b == B_FQ and p == 1:
                            project(l, B_FQ - 1, MLA, 3)
                attend(l, B_FG, FOX)
                for c in range(CHUNKS):
                    for p in units(l, B_OUT + c):
                        if c == 0 and p == 1:
                            project(l, B_OUT - 1, FOX, 3)
                        if c == 0 and (p == 2 or p == 5):
                            rest_of_y(l, 2 + p // 5)
                        if c and p == 1:
                            if c == 1:
                                dve.wait_ge(x_back, 16 * l + 16)
                            add_out(l, c - 1)
                add_out(l, CHUNKS - 1)
                link.close()
            link.n = 0
            dve.wait_ge(fin_in, 16)
            for c in range(CHUNKS):
                at = slice(c * CW, (c + 1) * CW)
                if c == CHUNKS - 1:
                    norm_factor(DEPTH, ("x",), D)
                last = dve.tensor_tensor(xy[:, :, at], xy[:, :, at],
                                         fin_g[:, at].unsqueeze(1).broadcast_to([P, TT, CW]), ALU.mult)
            link(DEPTH, last)
            newton(DEPTH, ("x",))
            for c in range(CHUNKS):
                at = slice(c * CW, (c + 1) * CW)
                for t in range(TT):
                    last = dve.tensor_scalar(xy[:, t, at], xy[:, t, at], ms[:, 7, t:t + 1], None, ALU.mult)
                last.then_inc(out_ready, 1)


_INS = ["x", "norm_g", "w_in", "forget_b", "q_norm_g", "w_q_up", "kv_norm_g", "w_kv_up", "w_branch", "w_out",
        "final_norm_g"]


def weight_units(w_in, w_q_up, w_kv_up, w_branch, w_out):
    def bodies(w, width):
        l, rows, n = w.shape
        w = w.reshape(l, rows // (2 * P), 2, P, n // width, width).transpose(0, 4, 1, 3, 2, 5)
        return w.reshape(l, -1, UNITS, P, 2 * width)

    def cols(first, n):
        return w_in[:, :, first:first + n]

    def gate(b, first, n):
        return bodies(cols(C_SILU + b * BW + first * CW, n * CW), CW)

    def rest(b):
        return [bodies(cols(C_MERGE + b * D, D), CW), bodies(w_branch[:, b], CW)]

    wide = [bodies(cols(C_IQ, IDX_HEADS * IDX_DIM), CW), bodies(cols(C_DQ, 3 * BW), CW), gate(DSA, 0, 2), *rest(DSA),
            bodies(cols(C_CQ, 2 * LORA), CW), gate(MLA, 0, 1), bodies(w_kv_up, CW), gate(MLA, 1, 1), *rest(MLA),
            bodies(cols(C_FQ, 3 * BW), CW), gate(FOX, 0, 2), *rest(FOX), bodies(w_out, CW)]
    narrow = np.concatenate([cols(C_IK, N_KPE), cols(C_KPE, ROPE), cols(C_FG, HEADS)], 2)
    return {"w_wide": np.ascontiguousarray(np.concatenate(wide, 1)),
            "w_narrow": np.ascontiguousarray(bodies(narrow, NW)[:, 0]),
            "w_qup": np.ascontiguousarray(bodies(w_q_up, QCW)[:, 0])}


def rope_table(dim):
    half = dim // 2
    inv = np.float32(10000.0) ** (-np.arange(half, dtype=np.float32) / np.float32(half))
    ang = np.arange(SEQ, dtype=np.float32)[:, None] * inv[None, :].astype(np.float32)
    cos, sin = np.cos(ang), np.sin(ang)
    both = np.stack([np.concatenate([cos, cos], 1), np.concatenate([-sin, sin], 1)], 1)
    return np.ascontiguousarray(both.reshape(TT, P, 2, dim).transpose(1, 2, 0, 3).astype(np.float32))


def kernel(**inputs):
    import concourse.bacc as bacc
    from concourse.bass_utils import run_bass_kernel_spmd

    nc = bacc.Bacc("TRN2", target_bir_lowering=False, num_devices=1)
    r = np.arange(P)
    square = np.stack([r[:, None] == r[None, :], r[:, None] <= r[None, :],
                       np.where(r[:, None] < r[None, :], NEG, 0.0)], 1).astype(np.float32)
    negsel = -np.repeat(np.eye(HEADS, dtype=np.float32)[:, :, None], P, 2)
    given = {n: np.ascontiguousarray(inputs[n]) for n in _INS}
    given.update(weight_units(*(given.pop(n) for n in ("w_in", "w_q_up", "w_kv_up", "w_branch", "w_out"))))
    for n in ("norm_g", "q_norm_g", "kv_norm_g"):
        given[n] = np.ascontiguousarray(given[n].reshape(DEPTH, -1, P).transpose(0, 2, 1))
    given.update(rope128=rope_table(HD), rope64=rope_table(ROPE), square=square,
                 negsel=np.ascontiguousarray(negsel))
    args = {n: nc.dram_tensor(f"in_{n}", a.shape, F32, kind="ExternalInput").ap() for n, a in given.items()}
    out = nc.dram_tensor("out", (1, SEQ, D), F32, kind="ExternalOutput").ap()
    build(nc, out=out, **args)
    r = run_bass_kernel_spmd(nc, [{f"in_{n}": a for n, a in given.items()}], core_ids=[0])
    return r.results[0]["out"]
```

```python
from contextlib import ExitStack

import numpy as np

import concourse.bass as bass
from concourse import mybir

F32 = mybir.dt.float32
F32R = mybir.dt.float32r
ALU = mybir.AluOpType
ACT = mybir.ActivationFunctionType
AX_X = mybir.AxisListType.X

P = 128
SEQ, D, DEPTH = 256, 2048, 2
TT = SEQ // P
KT = D // P
HEADS, HD = 8, 128
BW = HEADS * HD
IDX_HEADS, IDX_DIM = 16, 64
N_SEL = min(256, SEQ // 4)
LORA, ROPE = 512, 64
LT = LORA // P
QW = HD + ROPE
EPS = 1e-6
NEG = -1e30
TAKEN = -3e38
SCALE = HD ** -0.5
MLA_SCALE = QW ** -0.5
IDX_SCALE = (IDX_HEADS * IDX_DIM) ** -0.5

C_FQ, C_FG = 0, 3 * BW
C_DQ = C_FG + HEADS
C_IQ = C_DQ + 3 * BW
C_IK = C_IQ + IDX_HEADS * IDX_DIM
C_IW = C_IK + IDX_DIM
C_CQ = C_IW + IDX_HEADS
C_CKV = C_CQ + LORA
C_KPE = C_CKV + LORA
C_SILU = C_KPE + ROPE
C_MERGE = C_SILU + 3 * BW
D_IN = C_MERGE + 3 * D
FOX, DSA, MLA = 0, 1, 2

CW = 512
QCW = 2 * QW
N_IK, N_IW, N_KPE, N_FG = 0, 64, 80, 144
NW = N_FG + HEADS
UNITS = 8
RING = 4
TW = P + SEQ

B_IQ, B_NARROW, B_IQ1, B_DQ, B_DV = 0, 1, 2, 3, 7
B_DG = 9
B_CQ, B_CKV = 17, 18
B_MG0, B_QUP, B_KVUP, B_MG1 = 19, 20, 21, 22
B_FQ, B_FK, B_FV = 29, 31, 33
B_FG = 35
B_OUT = 43
BODIES = 47
LOW = 32
CUM_K = LOW + HEADS
U_LAYER = UNITS * BODIES
LOADS_LAYER = U_LAYER // RING
WIDE = [b for b in range(BODIES) if b not in (B_NARROW, B_QUP)]


class Order:

    def __init__(self, events, credit=0):
        self.at = {e: i for i, e in enumerate(events)}
        self.layer, self.credit = len(events), credit
        assert len(self.at) == len(events)

    def after(self, l, event):
        return l * self.layer + (self.at[event] + 1 + self.credit)

    def after_last(self, l, event):
        assert self.at[event] + self.credit >= self.layer
        return l * self.layer + (self.at[event] + 1 + self.credit - self.layer)

    def before(self, l, event):
        return l * self.layer + (self.at[event] + self.credit)


class Links:

    def __init__(self, engine, sem, layer):
        self.engine, self.sem, self.layer, self.n = engine, sem, layer, 0

    def __call__(self, l, ins):
        ins.then_inc(self.sem, 1)
        self.n += 1
        self.engine.wait_ge(self.sem, l * self.layer + self.n)

    def close(self):
        assert self.n == self.layer, (self.n, self.layer)


def head_pairs(branch):
    return [(branch, pair) for pair in range(HEADS // 2)]


def attention_fills(branch, pair):
    return [("scores", branch, pair), ("probs", branch, pair)]


AHEAD = 2
X_FILLS = Order(
    [("x", g) for g in range(AHEAD, 4)] + [("iq", 0), ("narrow",), ("cum",), ("iq", 1)]
    + [e for b in range(4) for e in (("index", 2 * b), ("qk", DSA, b), ("index", 2 * b + 1))]
    + [e for p in range(4) for e in attention_fills(DSA, p)]
    + [("code", 0), ("code", 1)] + [("q", j) for j in range(4)] + [("k", j) for j in range(3)]
    + [("scores", MLA, 0), ("k", 3), ("probs", MLA, 0)] + [e for p in range(1, 4) for e in attention_fills(MLA, p)]
    + [("qk", FOX, b) for b in range(4)] + [e for p in range(4) for e in attention_fills(FOX, p)]
    + [("y", g) for g in range(4)] + [("x", g) for g in range(AHEAD)], credit=AHEAD)
X_CREDIT = 1
PAIRS = Order(head_pairs(DSA) + head_pairs(MLA) + head_pairs(FOX))


def branch_chunks(branch, bank):
    return [("gate", branch, bank)] + [(m, branch, c) for m in ("merge", "proj") for c in range(bank, 4, 2)]


FREED = [
    Order([("v", DSA, 0)] + branch_chunks(DSA, 0) + [("gate", MLA, 0), ("q", 1), ("q", 3), ("k", 1), ("k", 3)]
          + branch_chunks(MLA, 0)[1:] + [("v", FOX, 0)] + branch_chunks(FOX, 0)[:-2]),
    Order([("v", DSA, 1)] + branch_chunks(DSA, 1) + [("q", 0), ("q", 2), ("k", 0), ("k", 2)]
          + branch_chunks(MLA, 1) + [("v", FOX, 1)] + branch_chunks(FOX, 1)[:-2]),
]
ROWS = [
    Order([("iq", 0), ("iq", 1), ("qk", DSA, 0), ("qk", DSA, 2), ("code", 0), ("q", 0), ("q", 2), ("k", 0),
           ("k", 2), ("qk", FOX, 0), ("qk", FOX, 2)]),
    Order([("narrow",), ("qk", DSA, 1), ("qk", DSA, 3), ("code", 1), ("q", 1), ("q", 3), ("k", 1), ("k", 3),
           ("qk", FOX, 1), ("qk", FOX, 3)]),
]
CHUNKS = 4
NORMS = Order([("x",), ("code", 0), ("code", 1)])
HALVED = Order([("x", g) for g in range(AHEAD, 4)] + [("iq", 0), ("narrow",), ("cum",), ("iq", 1)] + [("code", 0), ("code", 1)] + [("y", g) for g in range(4)]
               + [("x", g) for g in range(AHEAD)], credit=AHEAD)
TANHS = Order([("gate", b, c) for b in (DSA, MLA, FOX) for c in range(2)])
INDEX_PAIRS = Order([("index", i) for i in range(IDX_HEADS // 2)])
ACT_LINKS, DVE_LINKS = 4, 102


def parity(event):
    return next(i for i in range(2) if event in ROWS[i].at)


def build(nc, x, norms_g, w_wide, w_narrow, w_qup, forget_b, q_norm_g, kv_norm_g, final_norm_g, rope128,
          rope64, square, out):
    x_park = nc.dram_tensor("x_park", (P, TT, D), F32).ap()
    with ExitStack() as ctx:
        def sb(name, shape, dt=F32):
            return ctx.enter_context(nc.sbuf_tensor(name, shape, dt))

        def sem(name):
            return ctx.enter_context(nc.semaphore(name))

        raw = sb("raw", [P, RING, 2 * CW])
        w_hi = sb("w_hi", [P, RING, 2 * CW], F32R)
        w_lo = sb("w_lo", [P, RING, 2 * CW], F32R)
        h_hi = sb("h_hi", [P, KT, SEQ], F32R)
        h_lo = sb("h_lo", [P, KT, SEQ], F32R)
        o_hi = sb("o_hi", [P, HEADS, SEQ], F32R)
        o_lo = sb("o_lo", [P, HEADS, SEQ], F32R)
        xy = sb("xy", [P, TT, D])
        qkT = sb("qkT", [P, 2, HEADS, SEQ])
        vv = sb("vv", [P, TT, BW])
        gs = sb("gs", [P, TT, BW])
        th = sb("th", [P, TT, D])
        ev = sb("ev", [P, TT, CW])
        nat = sb("nat", [P, 2, TT, CW])
        ik_hi = sb("ik_hi", [P, SEQ], F32R)
        ik_lo = sb("ik_lo", [P, SEQ], F32R)
        kpT = sb("kpT", [P, SEQ])
        qrT = sb("qrT", [P, HEADS // 2, SEQ])
        score = sb("score", [P, TW])
        dbias = sb("dbias", [P, TW])
        top8 = sb("top8", [P, 2, 8])
        prob = sb("prob", [P, 2, TW])
        probT = sb("probT", [P, 2, TW])
        og = sb("og", [P, 2, TT, HD])
        iw = sb("iw", [P, TT, IDX_HEADS])
        lf = sb("lf", [P, 3, TT, HEADS])
        lg = sb("lg", [P, TT, CUM_K])
        cumq = sb("cumq", [P, TT, HEADS])
        cumT = sb("cumT", [CUM_K, SEQ], F32R)
        peak = sb("peak", [P, 2, 2, TT])
        sums = sb("sums", [P, 2, TT])
        rinv = sb("rinv", [P, 2, TT])
        sqp = sb("sqp", [P, TT, CHUNKS])
        ms = sb("ms", [P, 8, TT])
        xf = sb("xf", [P, 3, TT])
        rx128 = sb("rx128", [P, 2, TT, HD])
        rx64 = sb("rx64", [P, 2, TT, IDX_DIM])
        rp128 = sb("rp128", [P, 2, TT, HD])
        rp64 = sb("rp64", [P, 2, TT, IDX_DIM])
        sq = sb("sq", [P, 3, P])
        mask = sb("mask", [P, TW])
        ones = sb("ones", [P, P])
        picks = sb("picks", [CUM_K, HEADS])
        nsel = sb("nsel", [CUM_K, HEADS, P], F32R)
        g_h = sb("g_h", [P, KT])
        g_c = sb("g_c", [P, 2 * LT])
        fb = sb("fb", [P, HEADS])
        fin_g = gs[:, :, :].rearrange("p a n -> p (a n)")
        ident, tri, diag = sq[:, 0, :], sq[:, 1, :], sq[:, 2, :]

        G = ctx.enter_context(nc.psum_tensor("G", [P, 2, TT, CW], F32))
        X = ctx.enter_context(nc.psum_tensor("X", [P, 2, CW], F32))
        PV = ctx.enter_context(nc.psum_tensor("PV", [P, 2, TT, HD], F32))
        OT = ctx.enter_context(nc.psum_tensor("OT", [P, 2, SEQ], F32))
        XT = X[:, :, :].rearrange("p a n -> p (a n)")
        GT = G[:, 0, :, :].rearrange("p t n -> p (t n)")

        raw_ready = [sem(f"raw_ready{i}") for i in range(RING)]
        hi_ready = sem("hi_ready")
        unit_split = sem("unit_split")
        unit_done = sem("unit_done")
        freed = [sem("freed0"), sem("freed1")]
        rows_ready = [sem("rows_ready0"), sem("rows_ready1")]
        x_done = sem("x_done")
        x_used = sem("x_used")
        y_chunk = sem("y_chunk")
        x_chunk = sem("x_chunk")
        hi_taken = sem("hi_taken")
        squared = sem("squared")
        var_ready = sem("var_ready")
        root_ready = sem("root_ready")
        tanh_ready = sem("tanh_ready")
        nope_ready = sem("nope_ready")
        index_used = sem("index_used")
        fabs_ready, flog_ready, logf_ready = sem("fabs_ready"), sem("flog_ready"), sem("logf_ready")
        peak_ready, prob_ready = sem("peak_ready"), sem("prob_ready")
        pv_done, og_ready, ot_done, ot_hi, ot_used = (sem(n) for n in ("pv_done", "og_ready", "ot_done", "ot_hi",
                                                                       "ot_used"))
        x_load = [sem(f"x_load{c}") for c in range(CHUNKS)]
        x_back = [sem(f"x_back{c}") for c in range(CHUNKS)]
        x_parked = sem("x_parked")
        picks_ready = sem("picks_ready")
        square_in, consts_in = sem("square_in"), sem("consts_in")
        norm_in, params_in = sem("norm_in"), sem("params_in")
        waited = sem("waited")
        act_link, dve_link = sem("act_link"), sem("dve_link")
        fin_in, out_ready, out_stored = sem("fin_in"), sem("out_ready"), sem("out_stored")

        block = ctx.enter_context(nc.Block())

        x_v = x.rearrange("a (t p) d -> p (a t) d", p=P)
        o_v = out.rearrange("a (t p) d -> p (a t) d", p=P)
        TILES = ((0, P), (P, TW))

        @block.sync
        def _(sp):
            def load(l, b, src, width=CW):
                for p in range(UNITS):
                    sp.wait_ge(unit_split, l * U_LAYER + (UNITS * b + p + 1))
                    sp.dma_start(raw[:, p % RING, 0:2 * width], src[p]).then_inc(raw_ready[p % RING], 16)

            def load_wide(l, first, end):
                skipped = first - WIDE.index(first)
                with sp.Fori(first, end) as b:
                    load(l, b, w_wide[l, b - skipped])

            sp.dma_start(g_h[:, :], norms_g[0]).then_inc(norm_in, 16)
            sp.dma_start(sq[:, :, :], square).then_inc(square_in, 16)
            for c in range(CHUNKS - 1):
                sp.dma_start(xy[:, :, c * CW:(c + 1) * CW], x_v[:, :, c * CW:(c + 1) * CW]).then_inc(x_load[c], 16)
            with sp.Fori(0, DEPTH) as l:
                sp.wait_ge(y_chunk, CHUNKS * l + 1)
                sp.dma_start(g_c[:, 0:LT], q_norm_g[l]).then_inc(params_in, 16)
                sp.dma_start(g_c[:, LT:2 * LT], kv_norm_g[l]).then_inc(params_in, 16)
                sp.dma_start(fb[:, :], forget_b[l].unsqueeze(0).broadcast_to([P, HEADS])).then_inc(params_in, 16)
                load(l, B_IQ, w_wide[l, 0])
                load(l, B_NARROW, w_narrow[l], NW)
                load_wide(l, B_IQ1, B_DG)
                sp.wait_ge(x_done, X_FILLS.after(l, ("x", CHUNKS - 1)))
                sp.dma_start(x_park, xy[:, :, :]).then_inc(x_parked, 16)
                load_wide(l, B_DG, B_QUP)
                sp.wait_ge(x_used, X_FILLS.after(l, ("x", CHUNKS - 1)) + X_CREDIT)
                sp.dma_start(g_h[:, :], norms_g[l + 1]).then_inc(norm_in, 16)
                load(l, B_QUP, w_qup[l], QCW)
                load_wide(l, B_KVUP, B_OUT + 1)
                sp.wait_ge(x_done, X_FILLS.after(l, ("y", 3)))
                sp.wait_ge(x_parked, 16 * l + 16)
                for c in range(CHUNKS):
                    at = slice(c * CW, (c + 1) * CW)
                    sp.dma_start(xy[:, :, at], x_park[:, :, at]).then_inc(x_back[c], 16)
                    if c < CHUNKS - 1:
                        load(l, B_OUT + c + 1, w_wide[l, WIDE.index(B_OUT + c + 1)])
            sp.wait_ge(x_chunk, CHUNKS * DEPTH + 1)
            sp.dma_start(fin_g, final_norm_g.unsqueeze(0).broadcast_to([P, D])).then_inc(fin_in, 16)
            for c in range(CHUNKS):
                at = slice(c * CW, (c + 1) * CW)
                sp.wait_ge(out_ready, c + 1)
                sp.dma_start(o_v[:, :, at], xy[:, :, at]).then_inc(out_stored, 16)
            sp.wait_ge(out_stored, 16 * CHUNKS)

        @block.tensor
        def _(pe):
            def fill(l, event):
                pe.wait_ge(x_used, X_FILLS.before(l, event) + X_CREDIT)

            def units(l, b, width, plan, hi, lo):
                for p in range(UNITS):
                    ks, bank, start, stop, before = plan(p)
                    if start and before:
                        pe.wait_ge(*before)
                    pe.wait_ge(unit_split, l * U_LAYER + (UNITS * b + p + 1 + RING))
                    for i, k in enumerate(ks):
                        for t in range(TT):
                            dst = G[:, bank, t, 0:width]
                            at = slice(t * P, (t + 1) * P)
                            cols = slice(i * width, (i + 1) * width)
                            wh, wl = w_hi[:, p % RING, cols], w_lo[:, p % RING, cols]
                            pe.matmul(dst, hi[:, k, at], wh, start=start and i == 0, stop=False)
                            pe.matmul(dst, hi[:, k, at], wl, start=False, stop=False)
                            mm = pe.matmul(dst, lo[:, k, at], wh, start=False, stop=stop and i == 1)
                    mm.then_inc(unit_done, 1)
                    yield p

            def out_of(l, bank, *event):
                if event[:2] == ("proj", FOX):
                    return y_chunk, CHUNKS * l + event[2] + 2
                return freed[bank], FREED[bank].after(l, event)

            def w_in_units(l, b, bank, before, width=CW):
                return units(l, b, width, lambda p: ((2 * p, 2 * p + 1), bank, p == 0, p == UNITS - 1, before),
                             h_hi, h_lo)

            def proj_units(l, b, branch, c0):
                def plan(p):
                    c = c0 + p // 4
                    before = out_of(l, c % 2, *(("merge", branch, c + 2) if c < 2 else ("proj", branch, c - 2)))
                    return (2 * (p % 4), 2 * (p % 4) + 1), c % 2, p % 4 == 0, p % 4 == 3, before
                return units(l, b, CW, plan, o_hi, o_lo)

            def up_units(l, b, base, width, before):
                def plan(p):
                    return ((base + 2 * (p % 2), base + 2 * (p % 2) + 1), 1 - p // 2 % 2, p % 2 == 0, p % 2 == 1,
                            before[p // 2])
                return units(l, b, width, plan, o_hi, o_lo)

            def transposes(l, event, blocks):
                i = parity(event)
                pe.wait_ge(rows_ready[i], ROWS[i].after(l, event))
                fill(l, event)
                for j in range(blocks):
                    for t in range(TT):
                        mm = pe.transpose(XT[:, j * SEQ + t * P:j * SEQ + (t + 1) * P],
                                          nat[:, i, t, j * P:(j + 1) * P], ident)
                mm.then_inc(x_done, 1)

            def index_scores(l, pair):
                fill(l, ("index", pair))
                for e in range(2):
                    r = slice(IDX_DIM * e, IDX_DIM * (e + 1))
                    for t, (a, z) in enumerate(TILES):
                        at, keys, dst = slice(t * P, (t + 1) * P), slice(0, (t + 1) * P), X[:, e, a:z]
                        pe.matmul(dst, o_hi[r, pair, at], ik_hi[r, keys], start=True, stop=False)
                        pe.matmul(dst, o_hi[r, pair, at], ik_lo[r, keys], start=False, stop=False)
                        mm = pe.matmul(dst, o_lo[r, pair, at], ik_hi[r, keys], start=False, stop=True)
                mm.then_inc(x_done, 1)

            def scores(l, branch, pair):
                fill(l, ("scores", branch, pair))
                for e in range(2):
                    h = 2 * pair + e
                    for t, (a, z) in enumerate(TILES):
                        at, keys, dst = slice(t * P, (t + 1) * P), slice(0, (t + 1) * P), X[:, e, a:z]
                        mm = pe.matmul(dst, qkT[:, 0, h, at], qkT[:, 1, h, keys], start=True, stop=branch == DSA)
                        if branch == MLA:
                            r = slice(ROPE * e, ROPE * (e + 1))
                            mm = pe.matmul(dst, qrT[r, pair, at], kpT[r, keys], start=False, stop=True)
                        if branch == FOX:
                            mm = pe.matmul(dst, nsel[:, h, :], cumT[:, keys], start=False, stop=True)
                mm.then_inc(x_done, 1)

            def turn_probs(l, branch, pair):
                pe.wait_ge(prob_ready, PAIRS.after(l, (branch, pair)))
                fill(l, ("probs", branch, pair))
                for e in range(2):
                    for j in range(3):
                        mm = pe.transpose(X[:, e, j * P:(j + 1) * P], prob[:, e, j * P:(j + 1) * P], ident)
                mm.then_inc(x_done, 1)

            def values(l, branch, pair):
                pe.wait_ge(x_used, X_FILLS.after(l, ("probs", branch, pair)) + X_CREDIT)
                for e in range(2):
                    h = slice((2 * pair + e) * HD, (2 * pair + e + 1) * HD)
                    pe.matmul(PV[:, e, 0, :], probT[:, e, 0:P], vv[:, 0, h], start=True, stop=True)
                    pe.matmul(PV[:, e, 1, :], probT[:, e, P:2 * P], vv[:, 0, h], start=True, stop=False)
                    mm = pe.matmul(PV[:, e, 1, :], probT[:, e, 2 * P:TW], vv[:, 1, h], start=False, stop=True)
                mm.then_inc(pv_done, 1)

            def turn_heads(l, branch, pair):
                pe.wait_ge(og_ready, PAIRS.after(l, (branch, pair)))
                pe.wait_ge(ot_used, PAIRS.before(l, (branch, pair)) + 1)
                for e in range(2):
                    for t in range(TT):
                        mm = pe.transpose(OT[:, e, t * P:(t + 1) * P], og[:, e, t, :], ident)
                mm.then_inc(ot_done, 1)

            def attend(l, b, branch, first=0):
                for c in range(first, 2):
                    before = ("k", 2) if branch == MLA else ("v", branch, c)
                    for p in w_in_units(l, b, c, out_of(l, c, *before)):
                        if branch == MLA and p == 0:
                            transposes(l, ("k", 2), 2)
                        if branch == MLA and p == 3:
                            transposes(l, ("k", 3), 2)
                        if c == 1 and p == 1:
                            scores(l, branch, 0)
                        if c == 1 and p == 5:
                            turn_probs(l, branch, 0)
                    b += 1
                for c in range(4):
                    before = ("merge", branch, c - 2) if c > 1 else ("gate", branch, c)
                    if branch == MLA and c == 0:
                        before = ("k", 3)
                    for p in w_in_units(l, b, c % 2, out_of(l, c % 2, *before)):
                        if p == 0:
                            values(l, branch, c)
                        if p == 1 and c < 3:
                            scores(l, branch, c + 1)
                        if p == 3:
                            turn_heads(l, branch, c)
                        if p == 5 and c < 3:
                            turn_probs(l, branch, c + 1)
                    b += 1
                pe.wait_ge(ot_used, PAIRS.after(l, (branch, 3)) + 1)
                for c in (0, 2):
                    for p in proj_units(l, b + c // 2, branch, c):
                        if branch == FOX and c and p in (1, 4, 7):
                            turn_four(l, "y", p // 3)

            def turn_four(l, name, g, dst=XT):
                if name == "y":
                    pe.wait_ge(y_chunk, CHUNKS * l + (g + 2))
                else:
                    ahead = CHUNKS if g < AHEAD else 0
                    pe.wait_ge(x_load[g], 16)
                    pe.wait_ge(x_chunk, CHUNKS * l + (ahead + g + 1))
                if dst is XT:
                    fill(l, (name, g))
                for j in range(4):
                    for t in range(TT):
                        k = 4 * g + j
                        mm = pe.transpose(dst[:, j * SEQ + t * P:j * SEQ + (t + 1) * P],
                                          xy[:, t, k * P:(k + 1) * P], ident)
                mm.then_inc(x_done, 1)

            def halves(l, name):
                pe.wait_ge(x_used, X_FILLS.after(l, (name, 3)) + X_CREDIT)

            pe.sem_inc(unit_done, RING)
            pe.wait_ge(square_in, 16)
            for g in range(AHEAD):
                turn_four(-1, "x", g, (XT, GT)[g])
            with pe.Fori(0, DEPTH) as l:
                turn_four(l, "x", 2)
                for p in w_in_units(l, B_IQ, 1, None):
                    if p == 2:
                        turn_four(l, "x", 3)
                    if p == 5:
                        halves(l, "x")
                for p in w_in_units(l, B_NARROW, 0, None, NW):
                    pass
                for p in w_in_units(l, B_IQ1, 1, None):
                    if p == 0:
                        transposes(l, ("iq", 0), 4)
                    if p == 3:
                        transposes(l, ("narrow",), 2)
                    if p == 6:
                        pe.wait_ge(logf_ready, l + 1)
                        fill(l, ("cum",))
                        pe.matmul(X[:, 0, 0:HEADS], tri, lg[:, 0, 0:HEADS], start=True, stop=True)
                        pe.matmul(X[:, 0, HEADS:2 * HEADS], ones[:, :], lg[:, 0, 0:HEADS], start=True, stop=False)
                        pe.matmul(X[:, 0, HEADS:2 * HEADS], tri, lg[:, 1, 0:HEADS], start=False, stop=True)
                        pe.matmul(X[0:CUM_K, 1, 0:P], lg[:, 0, :], tri, start=True, stop=True)
                        pe.matmul(X[0:CUM_K, 1, P:SEQ], lg[:, 0, :], ones[:, :], start=True, stop=False)
                        mm = pe.matmul(X[0:CUM_K, 1, P:SEQ], lg[:, 1, :], tri, start=False, stop=True)
                        mm.then_inc(x_done, 1)
                for b in range(B_DQ, B_DG):
                    n = b - B_DQ - 1
                    for p in w_in_units(l, b, (b - B_DQ) % 2, None):
                        if n >= 0 and n < 4 and p == 0:
                            index_scores(l, 2 * n)
                        if n < 4 and p == 3:
                            transposes(l, ("qk", DSA, n) if n >= 0 else ("iq", 1), 4)
                        if n >= 0 and n < 4 and p == 5:
                            index_scores(l, 2 * n + 1)
                attend(l, B_DG, DSA)
                for p in w_in_units(l, B_CQ, 0, out_of(l, 0, "proj", DSA, 2)):
                    pass
                for i, (b, before) in enumerate(((B_CKV, out_of(l, 1, "proj", DSA, 3)), (B_MG0, None))):
                    for p in w_in_units(l, b, 1 - i, before):
                        if p == 5:
                            transposes(l, ("code", i), 4)
                pe.wait_ge(x_used, X_FILLS.after(l, ("code", 1)) + X_CREDIT)
                for p in up_units(l, B_QUP, 0, QCW, (None, out_of(l, 0, "gate", MLA, 0), out_of(l, 1, "q", 0),
                                                       out_of(l, 0, "q", 1))):
                    if p == 4 or p == 6:
                        transposes(l, ("q", p // 2 - 2), 3)
                for p in up_units(l, B_KVUP, LT, CW, (out_of(l, 1, "q", 2), out_of(l, 0, "q", 3), out_of(l, 1, "k", 0),
                                                       out_of(l, 0, "k", 1))):
                    if p == 0 or p == 2:
                        transposes(l, ("q", p // 2 + 2), 3)
                    if p == 4 or p == 6:
                        transposes(l, ("k", p // 2 - 2), 2)
                attend(l, B_MG1, MLA, first=1)
                for b in range(B_FQ, B_FG):
                    n = b - B_FQ - 1
                    before = out_of(l, n + 1, "proj", MLA, n + 3) if n < 1 else None
                    for p in w_in_units(l, b, (b - B_FQ) % 2, before):
                        if 0 <= n < 4 and p == 3:
                            transposes(l, ("qk", FOX, n), 4)
                attend(l, B_FG, FOX)
                for c in range(CHUNKS):
                    before = (x_chunk, CHUNKS * l + (CHUNKS + c - 1)) if c > 1 else out_of(l, c, "proj", FOX, 2 + c)
                    for p in w_in_units(l, B_OUT + c, c % 2, before):
                        if c == 0 and p == 3:
                            turn_four(l, "y", 3)
                        if c == 0 and p == 5:
                            halves(l, "y")
                        if c == CHUNKS - 1 and (p == 2 or p == 5):
                            turn_four(l, "x", p // 3)

        @block.scalar
        def _(act):
            link = Links(act, act_link, ACT_LINKS)

            def units(l, b, width=CW):
                for p in range(UNITS):
                    act.wait_ge(raw_ready[p % RING], l * (16 * LOADS_LAYER) + 16 * (2 * b + p // RING + 1))
                    act.wait_ge(unit_done, l * U_LAYER + (UNITS * b + p + 1))
                    act.copy(w_hi[:, p % RING, 0:2 * width], raw[:, p % RING, 0:2 * width]).then_inc(hi_ready, 1)
                    yield p

            def chunk_in(l, b, p=UNITS - 1):
                act.wait_ge(unit_done, l * U_LAYER + (UNITS * b + p + 1 + RING))

            def filled(l, event):
                act.wait_ge(x_done, X_FILLS.after(l, event))

            def gate(l, b, branch, c):
                chunk_in(l, b)
                if c:
                    act.wait_ge(freed[0], FREED[0].after(l, ("gate", branch, 0)))
                for t in range(TT):
                    last = act.activation(ev[:, t, :], G[:, c, t, :], ACT.Tanh, scale=xf[:, 1, t:t + 1])
                last.then_inc(tanh_ready, 1)

            def merge(l, b, c):
                chunk_in(l, b)
                for t in range(TT):
                    last = act.activation(th[:, t, c * CW:(c + 1) * CW], G[:, c % 2, t, :], ACT.Tanh,
                                          scale=xf[:, 1, t:t + 1])
                last.then_inc(freed[c % 2], 1)

            def softmax(l, branch, pair):
                scale = MLA_SCALE if branch == MLA else SCALE
                act.wait_ge(peak_ready, PAIRS.after(l, (branch, pair)))
                for e in range(2):
                    for t, (a, z) in enumerate(TILES):
                        last = act.activation(prob[:, e, a:z], prob[:, e, a:z], ACT.Exp, scale=scale,
                                              bias=peak[:, 1, e, t:t + 1], accum_out=sums[:, e, t:t + 1])
                last.then_inc(prob_ready, 1)

            def take_probs(l, branch, pair):
                filled(l, ("probs", branch, pair))
                act.copy(probT[:, :, :], X[:, :, 0:TW]).then_inc(x_used, 1)

            def take_heads(l, branch, pair):
                act.wait_ge(ot_done, PAIRS.after(l, (branch, pair)))
                act.copy(o_hi[:, 2 * pair:2 * pair + 2, :], OT[:, :, :]).then_inc(ot_hi, 1)

            def scaled(dst, bank):
                for t in range(TT):
                    last = act.activation(dst[:, t, :], G[:, bank, t, :], ACT.Copy, scale=xf[:, 0, t:t + 1])
                return last

            def take_values(l, b, bank):
                chunk_in(l, b)
                scaled(vv[:, :, bank * CW:(bank + 1) * CW], bank).then_inc(freed[bank], 1)

            def latent_kv(l, b, j):
                chunk_in(l, b, 2 * j + 1)
                src = G[:, 1 - j % 2, :, :].rearrange("p t (e c d) -> p t e c d", e=2, c=2)
                for t in range(TT):
                    last = act.copy(nat[:, j % 2, t, 0:2 * HD].rearrange("p (e d) -> p e d", e=2), src[:, t, :, 0, :])
                last.then_inc(rows_ready[j % 2], 1)
                for t in range(TT):
                    last = act.copy(vv[:, t, 2 * j * HD:2 * (j + 1) * HD].rearrange("p (e d) -> p e d", e=2),
                                    src[:, t, :, 1, :])
                last.then_inc(freed[1 - j % 2], 1)

            def take_keys(l, j):
                filled(l, ("k", j))
                act.copy(qkT[:, 1, 2 * j:2 * j + 2, :], X[:, 0, :].rearrange("p (e t) -> p e t", e=2))\
                   .then_inc(x_used, 1)

            def latent_q(l, b, j):
                chunk_in(l, b, 2 * j + 1)
                for t in range(TT):
                    last = act.copy(nat[:, j % 2, t, 0:2 * HD].rearrange("p (e d) -> p e d", e=2),
                                    G[:, 1 - j % 2, t, 0:QCW].rearrange("p (e d) -> p e d", e=2)[:, :, 0:HD])
                last.then_inc(nope_ready, 1)

            def take_queries(l, j):
                filled(l, ("q", j))
                act.copy(qkT[:, 0, 2 * j:2 * j + 2, :], X[:, 0, :].rearrange("p (e t) -> p e t", e=2))
                act.copy(qrT[:, j, :], X[:, 1, 0:SEQ]).then_inc(x_used, 1)

            def take_four(l, event, dst):
                filled(l, event)
                act.copy(dst, X[:, :, :].rearrange("p a (h t) -> p (a h) t", h=2)).then_inc(x_used, 1)

            def attend(l, b, branch, first=0):
                for c in range(first, 2):
                    for p in units(l, b):
                        if branch != MLA and p == 1:
                            if c == 0:
                                take_values(l, b - 1, 1)
                            else:
                                gate(l, b - 1, branch, 0)
                        if branch == MLA and p == 1:
                            take_keys(l, 2)
                            latent_kv(l, b - 1, 3)
                        if c == 1 and p == 4:
                            softmax(l, branch, 0)
                        if branch == MLA and p == 5:
                            take_keys(l, 3)
                        if c == 1 and p == 7:
                            take_probs(l, branch, 0)
                    b += 1
                for c in range(4):
                    for p in units(l, b):
                        if p == 1:
                            if c == 0:
                                gate(l, b - 1, branch, 1)
                            else:
                                merge(l, b - 1, c - 1)
                        if p == 4 and c < 3:
                            softmax(l, branch, c + 1)
                        if p == 5:
                            take_heads(l, branch, c)
                        if p == 7 and c < 3:
                            take_probs(l, branch, c + 1)
                    b += 1
                for c in range(2):
                    for p in units(l, b + c):
                        if c == 0 and p == 1:
                            merge(l, b - 1, 3)
                        if branch == FOX and c == 1 and (p == 3 or p == 6):
                            take_y(l, p // 3 - 1)

            def root(l, event):
                act.wait_ge(var_ready, NORMS.after(l, event))
                link(l, act.activation(ms[:, 2, :], ms[:, 1, :], ACT.Ln))
                act.activation(ms[:, 3, :], ms[:, 2, :], ACT.Exp, scale=-0.5).then_inc(root_ready, 1)

            def take_upper(l, event, hi, g=None, src=XT):
                filled(l, event)
                if g is None:
                    last = act.copy(hi, X[:, :, :].rearrange("p a (h t) -> p (a h) t", h=2))
                else:
                    for j in range(4):
                        last = act.activation(hi[:, j, :], src[:, j * SEQ:(j + 1) * SEQ], ACT.Copy,
                                              scale=g[:, j:j + 1])
                last.then_inc(hi_taken, 1)

            def take_x(l, g, src=XT):
                take_upper(l, ("x", g), h_hi[:, 4 * g:4 * g + 4, :], g_h[:, 4 * g:4 * g + 4], src)

            def take_y(l, g):
                take_upper(l, ("y", g), h_hi[:, 4 * g:4 * g + 4, :])

            def squares(l, c):
                for t in range(TT):
                    last = act.activation(th[:, t, c * CW:(c + 1) * CW], xy[:, t, c * CW:(c + 1) * CW], ACT.Square,
                                          accum_out=sqp[:, t, c:c + 1])
                return last

            act.wait_ge(square_in, 16)
            act.activation(mask[:, 0:P], diag, ACT.Copy)
            act.activation(mask[:, P:2 * P], diag, ACT.Copy, scale=0.0)
            act.activation(mask[:, 2 * P:TW], diag, ACT.Copy)
            act.wait_ge(norm_in, 16)
            take_x(-1, 0)
            at = slice((CHUNKS - 1) * CW, D)
            act.dma_start(xy[:, :, at], x_v[:, :, at]).then_inc(x_load[CHUNKS - 1], 16)
            act.dma_start(rp128[:, :, :, :], rope128).then_inc(consts_in, 16)
            act.dma_start(rp64[:, :, :, :], rope64).then_inc(consts_in, 16)
            take_x(-1, 1, GT)
            with act.Fori(0, DEPTH) as l:
                for p in units(l, B_IQ):
                    if p == 0 or p == 4:
                        take_x(l, 2 + p // 4)
                    if p == 2:
                        squares(l, 0)
                    if p == 3 or p == 5:
                        squares(l, p // 2)
                    if p == 6:
                        squares(l, 3).then_inc(squared, 1)
                    if p == 7:
                        root(l, ("x",))
                for p in units(l, B_NARROW, NW):
                    pass
                for p in units(l, B_IQ1):
                    if p == 2:
                        take_upper(l, ("iq", 0), o_hi[:, 0:4, :])
                    if p == 3:
                        act.wait_ge(fabs_ready, l + 1)
                        link(l, act.activation(lf[:, 2, :, :], lf[:, 1, :, :], ACT.Exp, scale=-1.0))
                        act.activation(lf[:, 2, :, :], lf[:, 2, :, :], ACT.Ln, bias=1.0).then_inc(flog_ready, 1)
                    if p == 5:
                        filled(l, ("narrow",))
                        act.copy(ik_hi[:, :], X[:, 0, 0:SEQ])
                        act.copy(kpT[:, :], X[:, 0, SEQ:2 * SEQ]).then_inc(hi_taken, 1)
                    if p == 7:
                        filled(l, ("cum",))
                        act.activation(cumT[:, :], X[0:CUM_K, 1, 0:SEQ], ACT.Copy, scale=1 / SCALE)\
                           .then_inc(hi_taken, 1)
                for b in range(B_DQ, B_DG):
                    n = b - B_DQ - 1
                    for p in units(l, b):
                        if b == B_DV + 1 and p == 1:
                            take_values(l, b - 1, 0)
                        if 0 <= n < 4 and (p == 2 or p == 7):
                            pair = 2 * n + (p == 7)
                            filled(l, ("index", pair))
                            act.wait_ge(index_used, INDEX_PAIRS.before(l, ("index", pair)) + 1)
                            act.activation(prob[:, :, :], X[:, :, 0:TW], ACT.Relu).then_inc(x_used, 1)
                        if n < 4 and p == 5:
                            if n < 0:
                                take_upper(l, ("iq", 1), o_hi[:, 4:8, :])
                            else:
                                take_four(l, ("qk", DSA, n), qkT[:, n // 2, 4 * (n % 2):4 * (n % 2) + 4, :])
                attend(l, B_DG, DSA)
                for p in units(l, B_CQ):
                    pass
                for i, b in enumerate((B_CKV, B_MG0)):
                    for p in units(l, b):
                        if p == 1:
                            chunk_in(l, b - 1)
                            for t in range(TT):
                                last = act.activation((prob, probT)[t][:, :, 0:CW // 2],
                                                      G[:, i, t, :].rearrange("p (a n) -> p a n", a=2), ACT.Square,
                                                      accum_out=ms[:, 0, t:t + 1])
                            last.then_inc(squared, 1)
                        if p == 3:
                            root(l, ("code", i))
                        if p == 7:
                            take_upper(l, ("code", i), o_hi[:, LT * i:LT * (i + 1), :], g_c[:, LT * i:LT * (i + 1)])
                for p in units(l, B_QUP, QCW):
                    if p == 1:
                        gate(l, B_MG0, MLA, 0)
                    if p in (3, 5, 7):
                        latent_q(l, B_QUP, (p - 3) // 2)
                    if p == 6:
                        take_queries(l, 0)
                for p in units(l, B_KVUP):
                    if p == 0 or p == 2 or p == 4:
                        take_queries(l, 1 + p // 2)
                    if p == 1:
                        latent_q(l, B_QUP, 3)
                    if p == 3 or p == 5:
                        latent_kv(l, B_KVUP, (p - 3) // 2)
                    if p == 6:
                        take_keys(l, 0)
                    if p == 7:
                        latent_kv(l, B_KVUP, 2)
                        take_keys(l, 1)
                attend(l, B_MG1, MLA, first=1)
                for b in range(B_FQ, B_FG):
                    n = b - B_FQ - 1
                    for p in units(l, b):
                        if 0 <= n < 4 and p == 1:
                            chunk_in(l, b - 1)
                            scaled(nat[:, n % 2, :, :], n % 2).then_inc(rows_ready[n % 2], 1)
                        if n == 4 and p == 1:
                            take_values(l, b - 1, 0)
                        if 0 <= n < 4 and p == 5:
                            take_four(l, ("qk", FOX, n), qkT[:, n // 2, 4 * (n % 2):4 * (n % 2) + 4, :])
                attend(l, B_FG, FOX)
                for c in range(CHUNKS):
                    for p in units(l, B_OUT + c):
                        if c == 0 and (p == 2 or p == 5):
                            take_y(l, 2 + p // 5)
                        if c == CHUNKS - 1 and (p == 4 or p == 7):
                            if p == 4:
                                act.wait_ge(norm_in, 16 * l + 32)
                            take_x(l, p // 5)
                link.close()
            act.wait_ge(x_chunk, CHUNKS * DEPTH + CHUNKS - 1)
            for c in range(CHUNKS - 1):
                squares(DEPTH, c)
            act.wait_ge(x_chunk, CHUNKS * DEPTH + CHUNKS)
            squares(DEPTH, CHUNKS - 1).then_inc(squared, 1)
            act.wait_ge(var_ready, NORMS.layer * DEPTH + 1)
            act.activation(ms[:, 2, :], ms[:, 1, :], ACT.Ln).then_inc(act_link, 1)
            act.wait_ge(act_link, ACT_LINKS * DEPTH + 1)
            act.activation(ms[:, 3, :], ms[:, 2, :], ACT.Exp, scale=-0.5).then_inc(root_ready, 1)

        @block.vector
        def _(dve):
            link = Links(dve, dve_link, DVE_LINKS)

            def units(l, b, width=CW):
                for p in range(UNITS):
                    dve.wait_ge(hi_ready, l * U_LAYER + (UNITS * b + p + 1))
                    r = p % RING
                    dve.tensor_tensor(w_lo[:, r, 0:2 * width], raw[:, r, 0:2 * width],
                                      w_hi[:, r, 0:2 * width].bitcast(F32), ALU.subtract).then_inc(unit_split, 1)
                    yield p

            def chunk_in(l, b, p=UNITS - 1):
                dve.wait_ge(unit_done, l * U_LAYER + (UNITS * b + p + 1 + RING))

            def filled(l, event):
                dve.wait_ge(x_done, X_FILLS.after(l, event))

            def rotate(l, t1, src, dst, table, heads, dim, tiles=range(TT)):
                half = dim // 2
                for t in tiles:
                    cos = table[:, 0, t, :].unsqueeze(1).broadcast_to([P, heads, dim])
                    dve.tensor_tensor(t1[:, t], src[:, t], cos, ALU.mult)
                    sin = table[:, 1, t, :].unsqueeze(1).broadcast_to([P, heads, dim])
                    dve.tensor_tensor(dst[:, t, :, 0:half], src[:, t, :, half:dim], sin[:, :, 0:half], ALU.mult)
                    last = dve.tensor_tensor(dst[:, t, :, half:dim], src[:, t, :, 0:half], sin[:, :, half:dim],
                                             ALU.mult)
                return last

            def rotate_chunk(l, b, bank, i, table, heads, dim, part=None):
                if part in (None, 0):
                    chunk_in(l, b)
                src = G[:, bank, :, :].rearrange("p t (h d) -> p t h d", h=heads)
                t1 = ev[:, :, :].rearrange("p t (h d) -> p t h d", h=heads)
                dst = nat[:, i, :, :].rearrange("p t (h d) -> p t h d", h=heads)
                if part is None:
                    link(l, rotate(l, t1, src, dst, table, heads, dim))
                elif part < TT:
                    last = rotate(l, t1, src, dst, table, heads, dim, (part,))
                    if part == TT - 1:
                        link(l, last)
                if part in (None, TT):
                    dve.tensor_tensor(nat[:, i, :, :], nat[:, i, :, :], ev[:, :, :], ALU.add)\
                       .then_inc(rows_ready[i], 1)

            def norm_factor(l, event, width):
                dve.wait_ge(squared, NORMS.after(l, event))
                if event == ("x",):
                    link(l, dve.tensor_reduce(ms[:, 0, :], sqp[:, :, :], AX_X, ALU.add))
                if event != ("x",):
                    link(l, dve.tensor_tensor(ms[:, 0, :], ms[:, 0, :], xf[:, 2, :], ALU.mult))
                dve.tensor_scalar(ms[:, 1, :], ms[:, 0, :], 1.0 / width, EPS, ALU.mult, ALU.add)\
                   .then_inc(var_ready, 1)

            def newton(l, event):
                dve.wait_ge(root_ready, NORMS.after(l, event))
                link(l, dve.tensor_tensor(ms[:, 4, :], ms[:, 3, :], ms[:, 3, :], ALU.mult))
                link(l, dve.tensor_tensor(ms[:, 5, :], ms[:, 4, :], ms[:, 1, :], ALU.mult))
                link(l, dve.tensor_scalar(ms[:, 6, :], ms[:, 5, :], -0.5, 1.5, ALU.mult, ALU.add))
                link(l, dve.tensor_tensor(ms[:, 7, :], ms[:, 3, :], ms[:, 6, :], ALU.mult))
                if event != ("x",):
                    link(l, dve.tensor_tensor(ms[:, 7, :], ms[:, 7, :], xf[:, 0, :], ALU.mult))

            def take_lower(l, event, hi, lo, g=None, src=XT):
                dve.wait_ge(hi_taken, HALVED.after(l, event))
                filled(l, event)
                if g is None:
                    if src is XT:
                        src = X[:, :, :].rearrange("p a (h t) -> p (a h) t", h=2)
                    last = dve.tensor_tensor(lo, src, hi.bitcast(F32), ALU.subtract)
                else:
                    for j in range(4):
                        last = dve.scalar_tensor_tensor(out=lo[:, j, :], in0=src[:, j * SEQ:(j + 1) * SEQ],
                                                        scalar=g[:, j:j + 1], in1=hi[:, j, :].bitcast(F32),
                                                        op0=ALU.mult, op1=ALU.subtract)
                last.then_inc(x_used, 1)

            def gate(l, branch, c):
                dve.wait_ge(tanh_ready, TANHS.after(l, ("gate", branch, c)))
                dve.scalar_tensor_tensor(out=gs[:, :, c * CW:(c + 1) * CW], in0=ev[:, :, :], scalar=1.0,
                                         in1=G[:, c, :, :], op0=ALU.add, op1=ALU.mult).then_inc(freed[c], 1)

            def logits(l, branch, pair):
                filled(l, ("scores", branch, pair))
                if branch == FOX:
                    for e in range(2):
                        for t, (a, z) in enumerate(TILES):
                            h = 2 * pair + e
                            last = dve.scalar_tensor_tensor(out=prob[:, e, a:z], in0=X[:, e, a:z],
                                                            scalar=cumq[:, t, h:h + 1], in1=mask[:, a:z],
                                                            op0=ALU.add, op1=ALU.add)
                else:
                    bias = dbias if branch == DSA else mask
                    last = dve.tensor_tensor(prob[:, :, :], X[:, :, 0:TW],
                                             bias[:, :].unsqueeze(1).broadcast_to([P, 2, TW]), ALU.add)
                last.then_inc(x_used, 1)
                dve.wait_ge(x_used, X_FILLS.after(l, ("scores", branch, pair)) + X_CREDIT)
                for t, (a, z) in enumerate(TILES):
                    last = dve.tensor_reduce(peak[:, 0, :, t], prob[:, :, a:z], AX_X, ALU.max)
                link(l, last)
                scale = MLA_SCALE if branch == MLA else SCALE
                dve.tensor_scalar(peak[:, 1, :, :], peak[:, 0, :, :], -scale, None, ALU.mult).then_inc(peak_ready, 1)

            def gate_heads(l, branch, pair):
                dve.wait_ge(prob_ready, PAIRS.after(l, (branch, pair)))
                link(l, dve.reciprocal(rinv[:, :, :], sums[:, :, :]))
                link(l, dve.tensor_tensor(rinv[:, :, :], rinv[:, :, :],
                                          xf[:, 1, :].unsqueeze(1).broadcast_to([P, 2, TT]), ALU.mult))
                dve.wait_ge(pv_done, PAIRS.after(l, (branch, pair)))
                for e in range(2):
                    h = slice((2 * pair + e) * HD, (2 * pair + e + 1) * HD)
                    for t in range(TT):
                        last = dve.scalar_tensor_tensor(out=og[:, e, t, :], in0=PV[:, e, t, :],
                                                        scalar=rinv[:, e, t:t + 1], in1=gs[:, t, h],
                                                        op0=ALU.mult, op1=ALU.mult)
                last.then_inc(og_ready, 1)

            def rest_of_heads(l, branch, pair):
                dve.wait_ge(ot_hi, PAIRS.after(l, (branch, pair)))
                at = slice(2 * pair, 2 * pair + 2)
                dve.tensor_tensor(o_lo[:, at, :], OT[:, :, :], o_hi[:, at, :].bitcast(F32), ALU.subtract)\
                   .then_inc(ot_used, 1)

            def project(l, b, branch, c):
                chunk_in(l, b, 4 * (c % 2) + 3)
                if branch == DSA and c == 0:
                    dve.wait_ge(x_parked, 16 * l + 16)
                at = slice(c * CW, (c + 1) * CW)
                link(l, dve.scalar_tensor_tensor(out=ev[:, :, :], in0=th[:, :, at], scalar=1.0, in1=G[:, c % 2, :, :],
                                                 op0=ALU.add, op1=ALU.mult))
                if branch == DSA:
                    last = dve.tensor_scalar(xy[:, :, at], ev[:, :, :], 0.5, None, ALU.mult)
                else:
                    last = dve.scalar_tensor_tensor(out=xy[:, :, at], in0=ev[:, :, :], scalar=0.5, in1=xy[:, :, at],
                                                    op0=ALU.mult, op1=ALU.add)
                last.then_inc(y_chunk if branch == FOX else freed[c % 2], 1)

            def rest_of_x(l, g, src=XT):
                at = slice(4 * g, 4 * g + 4)
                take_lower(l, ("x", g), h_hi[:, at, :], h_lo[:, at, :], g_h[:, at], src)

            def rest_of_y(l, g):
                at = slice(4 * g, 4 * g + 4)
                take_lower(l, ("y", g), h_hi[:, at, :], h_lo[:, at, :])

            def add_out(l, c):
                chunk_in(l, B_OUT + c)
                dve.wait_ge(x_back[c], 16 * l + 16)
                at = slice(c * CW, (c + 1) * CW)
                dve.tensor_tensor(xy[:, :, at], G[:, c % 2, :, :], xy[:, :, at], ALU.add).then_inc(x_chunk, 1)

            def spread_factor(l):
                dve.tensor_scalar(xf[:, 0, :], ms[:, 7, :], 1.0, None, ALU.mult)
                dve.tensor_scalar(xf[:, 1, :], ms[:, 7, :], 0.5, None, ALU.mult)
                dve.tensor_tensor(xf[:, 2, :], ms[:, 7, :], ms[:, 7, :], ALU.mult)
                dve.wait_ge(consts_in, 32)
                for src, dst in ((rp128, rx128), (rp64, rx64)):
                    for t in range(TT):
                        last = dve.tensor_scalar(dst[:, :, t, :], src[:, :, t, :], ms[:, 7, t:t + 1], None, ALU.mult)
                link(l, last)

            def attend(l, b, branch, first=0):
                for c in range(first, 2):
                    for p in units(l, b):
                        if branch == DSA and c == 0 and p == 2:
                            link(l, dve.tensor_scalar(dbias[:, :], score[:, :], TAKEN / 1.5, NEG, ALU.is_gt, ALU.mult))
                            link(l, dve.tensor_tensor(dbias[:, :], dbias[:, :], mask[:, :], ALU.add))
                        if branch != MLA and c == 1 and p == 1:
                            gate(l, branch, 0)
                        if c == 1 and p == 3:
                            logits(l, branch, 0)
                    b += 1
                for c in range(4):
                    for p in units(l, b):
                        if c == 0 and p == 1:
                            gate(l, branch, 1)
                        if p == 2:
                            gate_heads(l, branch, c)
                        if p == 3 and c < 3:
                            logits(l, branch, c + 1)
                        if p == 5:
                            rest_of_heads(l, branch, c)
                    b += 1
                for c in range(2):
                    for p in units(l, b + c):
                        if c == 1 and p == 1:
                            project(l, b, branch, 1)
                        if branch == FOX and c == 1 and p == 3:
                            rest_of_y(l, 0)
                        if p == 5:
                            project(l, b + c, branch, 2 * c)
                        if branch == FOX and c == 1 and p == 6:
                            rest_of_y(l, 1)

            def latent_q(l, b, j):
                dve.wait_ge(nope_ready, l * 4 + (j + 1))
                chunk_in(l, b, 2 * j + 1)
                src = G[:, 1 - j % 2, :, 0:QCW].rearrange("p t (e d) -> p t e d", e=2)[:, :, :, HD:QW]
                dst = nat[:, j % 2, :, 2 * HD:3 * HD].rearrange("p t (e d) -> p t e d", e=2)
                t1 = ev[:, :, 0:HD].rearrange("p t (e d) -> p t e d", e=2)
                if j:
                    dve.wait_ge(rows_ready[(j - 1) % 2], ROWS[(j - 1) % 2].after(l, ("q", j - 1)))
                else:
                    dve.wait_ge(freed[0], FREED[0].after(l, ("gate", MLA, 0)))
                rotate(l, t1, src, dst, rp64, 2, ROPE).then_inc(freed[1 - j % 2], 1)
                dve.wait_ge(freed[1 - j % 2], FREED[1 - j % 2].after(l, ("q", j)))
                dve.tensor_tensor(nat[:, j % 2, :, 2 * HD:3 * HD], nat[:, j % 2, :, 2 * HD:3 * HD], ev[:, :, 0:HD],
                                  ALU.add).then_inc(rows_ready[j % 2], 1)

            dve.sem_inc(unit_split, RING)
            dve.sem_inc(x_chunk, CHUNKS)
            dve.sem_inc(x_used, X_CREDIT)
            for free in (ot_used, index_used, y_chunk):
                dve.sem_inc(free, 1)
            dve.memset(ones[:, :], 1.0)
            dve.memset(ms[:, :, :], 1.0)
            dve.memset(lg[:, :, :], 0.0)
            dve.wait_ge(square_in, 16)
            dve.tensor_tensor(picks[:, :], ident[0:CUM_K, 0:HEADS], ident[0:CUM_K, LOW:CUM_K], ALU.add)\
               .then_inc(picks_ready, 1)
            dve.wait_ge(picks_ready, 1)
            dve.tensor_scalar(nsel[:, :, :], picks[:, :].unsqueeze(2).broadcast_to([CUM_K, HEADS, P]), -1.0, None,
                              ALU.mult)
            dve.wait_ge(norm_in, 16)
            for g in range(AHEAD):
                rest_of_x(-1, g, (XT, GT)[g])
            with dve.Fori(0, DEPTH) as l:
                for p in units(l, B_IQ):
                    if p == 1 or p == 4:
                        rest_of_x(l, 2 + p // 4)
                    if p == 6:
                        norm_factor(l, ("x",), D)
                for p in units(l, B_NARROW, NW):
                    if p == 0:
                        newton(l, ("x",))
                        spread_factor(l)
                    if p == 2 or p == 6:
                        rotate_chunk(l, B_IQ, 1, 0, rx64, 8, IDX_DIM, p // 4)
                for p in units(l, B_IQ1):
                    if p == 0:
                        rotate_chunk(l, B_IQ, 1, 0, rx64, 8, IDX_DIM, TT)
                    if p == 1:
                        chunk_in(l, B_NARROW)
                        z = G[:, 0, :, :]
                        dve.wait_ge(params_in, 48 * l + 48)
                        for t in range(TT):
                            factor = xf[:, 0, t:t + 1]
                            dve.tensor_scalar(iw[:, t, :], z[:, t, N_IW:N_KPE], factor, IDX_SCALE, ALU.mult, ALU.mult)
                            last = dve.scalar_tensor_tensor(out=lf[:, 0, t, :], in0=z[:, t, N_FG:NW], scalar=factor,
                                                            in1=fb[:, :], op0=ALU.mult, op1=ALU.add)
                        link(l, last)
                        src = z[:, :, 0:2 * N_KPE].rearrange("p t (e d) -> p t e d", e=2)[:, :, :, 0:ROPE]
                        dup = nat[:, 1, :, 0:2 * P].rearrange("p t (e c d) -> p t e c d", e=2, c=2)
                        t1 = ev[:, :, 0:P].rearrange("p t (e d) -> p t e d", e=2)
                        link(l, rotate(l, t1, src, dup[:, :, :, 0, :], rx64, 2, ROPE))
                        for t in range(TT):
                            dve.tensor_tensor(dup[:, t, :, 1, :], dup[:, t, :, 0, :], t1[:, t], ALU.add)
                        for t in range(TT):
                            last = dve.tensor_tensor(dup[:, t, :, 0, :], dup[:, t, :, 0, :], t1[:, t], ALU.add)
                        last.then_inc(rows_ready[1], 1)
                    if p == 2:
                        link(l, dve.tensor_scalar(lf[:, 1, :, :], lf[:, 0, :, :], -1.0, None, ALU.mult))
                        dve.tensor_tensor(lf[:, 1, :, :], lf[:, 1, :, :], lf[:, 0, :, :], ALU.max)\
                           .then_inc(fabs_ready, 1)
                    if p == 4:
                        dve.wait_ge(flog_ready, l + 1)
                        for at in (0, LOW):
                            last = dve.scalar_tensor_tensor(out=lg[:, :, at:at + HEADS], in0=lf[:, 0, :, :],
                                                            scalar=0.0, in1=lf[:, 2, :, :], op0=ALU.min,
                                                            op1=ALU.subtract)
                        last.then_inc(logf_ready, 1)
                    if p == 3:
                        take_lower(l, ("iq", 0), o_hi[:, 0:4, :], o_lo[:, 0:4, :])
                    if p == 6:
                        take_lower(l, ("narrow",), ik_hi[:, :], ik_lo[:, :], src=X[:, 0, 0:SEQ])
                    if p == 7:
                        dve.wait_ge(hi_taken, HALVED.after(l, ("cum",)))
                        filled(l, ("cum",))
                        dve.tensor_scalar(cumq[:, :, :], X[:, 0, 0:2 * HEADS].rearrange("p (t h) -> p t h", t=TT),
                                          1 / SCALE, None, ALU.mult)
                        low = slice(LOW, CUM_K)
                        dve.scalar_tensor_tensor(out=cumT[low, :], in0=X[low, 1, 0:SEQ], scalar=1 / SCALE,
                                                 in1=cumT[low, :].bitcast(F32), op0=ALU.mult, op1=ALU.subtract)\
                           .then_inc(x_used, 1)
                for b in range(B_DQ, B_DG):
                    n = b - B_DQ - 1
                    for p in units(l, b):
                        if b == B_DV + 1:
                            if p == 0:
                                link(l, dve.tensor_tensor(score[:, :], score[:, :], mask[:, :], ALU.add))
                            dve.sem_inc(waited, 1)
                            for t, (a, z) in enumerate(TILES):
                                last = dve.max(top8[:, t, :], score[:, a:z])
                            link(l, last)
                            dve.sem_inc(waited, 1)
                            for t, (a, z) in enumerate(TILES):
                                last = dve.match_replace(score[:, a:z], top8[:, t, :], score[:, a:z], TAKEN)
                            link(l, last)
                        if n < 0 and p == 7:
                            take_lower(l, ("iq", 1), o_hi[:, 4:8, :], o_lo[:, 4:8, :])
                        if n < 0 and p in (1, 2, 3):
                            rotate_chunk(l, b - 1, 1, 0, rx64, 8, IDX_DIM, p - 1)
                        if 0 <= n < 4 and p == 1:
                            rotate_chunk(l, b - 1, n % 2, n % 2, rx128, 4, HD)
                        if 0 <= n < 4 and (p == 2 or p == 7):
                            pair = 2 * n + (p == 7)
                            dve.wait_ge(x_used, X_FILLS.after(l, ("index", pair)) + X_CREDIT)
                            for e in range(2):
                                for t, (a, z) in enumerate(TILES):
                                    w = iw[:, t, 2 * pair + e:2 * pair + e + 1]
                                    if pair == 0 and e == 0:
                                        last = dve.tensor_scalar(score[:, a:z], prob[:, e, a:z], w, None, ALU.mult)
                                    else:
                                        last = dve.scalar_tensor_tensor(out=score[:, a:z], in0=prob[:, e, a:z],
                                                                        scalar=w, in1=score[:, a:z], op0=ALU.mult,
                                                                        op1=ALU.add)
                                if e == 0:
                                    link(l, last)
                            last.then_inc(index_used, 1)
                            dve.wait_ge(index_used, INDEX_PAIRS.after(l, ("index", pair)) + 1)
                attend(l, B_DG, DSA)
                for p in units(l, B_CQ):
                    if p == 1:
                        project(l, B_CQ - 1, DSA, 3)
                for i, b in enumerate((B_CKV, B_MG0)):
                    for p in units(l, b):
                        if p == 2:
                            norm_factor(l, ("code", i), LORA)
                        if p == 4:
                            newton(l, ("code", i))
                            for t in range(TT):
                                last = dve.tensor_scalar(nat[:, i, t, :], G[:, i, t, :], ms[:, 7, t:t + 1], None,
                                                         ALU.mult)
                            last.then_inc(rows_ready[i], 1)
                        if p == 7:
                            at = slice(LT * i, LT * (i + 1))
                            take_lower(l, ("code", i), o_hi[:, at, :], o_lo[:, at, :], g_c[:, at])
                for p in units(l, B_QUP, QCW):
                    if p == 1:
                        gate(l, MLA, 0)
                    if p in (3, 5, 7):
                        latent_q(l, B_QUP, (p - 3) // 2)
                for p in units(l, B_KVUP):
                    if p == 1:
                        latent_q(l, B_QUP, 3)
                attend(l, B_MG1, MLA, first=1)
                for b in range(B_FQ, B_FG):
                    for p in units(l, b):
                        if b == B_FQ and p == 1:
                            project(l, B_FQ - 1, MLA, 3)
                attend(l, B_FG, FOX)
                for c in range(CHUNKS):
                    for p in units(l, B_OUT + c):
                        if c == 0 and p == 1:
                            project(l, B_OUT - 1, FOX, 3)
                        if c == 0 and (p == 2 or p == 5):
                            rest_of_y(l, 2 + p // 5)
                        if c and p == 1:
                            add_out(l, c - 1)
                        if c == CHUNKS - 1 and p == 4:
                            dve.wait_ge(norm_in, 16 * l + 32)
                            rest_of_x(l, 0)
                rest_of_x(l, 1)
                add_out(l, CHUNKS - 1)
                link.close()
            link.n = 0
            norm_factor(DEPTH, ("x",), D)
            newton(DEPTH, ("x",))
            dve.wait_ge(fin_in, 16)
            for c in range(CHUNKS):
                at = slice(c * CW, (c + 1) * CW)
                for t in range(TT):
                    last = dve.scalar_tensor_tensor(out=xy[:, t, at], in0=xy[:, t, at], scalar=ms[:, 7, t:t + 1],
                                                    in1=fin_g[:, at], op0=ALU.mult, op1=ALU.mult)
                last.then_inc(out_ready, 1)


_INS = ["x", "norm_g", "w_in", "forget_b", "q_norm_g", "w_q_up", "kv_norm_g", "w_kv_up", "w_branch", "w_out",
        "final_norm_g"]


def weight_units(w_in, w_q_up, w_kv_up, w_branch, w_out):
    def bodies(w, width):
        l, rows, n = w.shape
        w = w.reshape(l, rows // (2 * P), 2, P, n // width, width).transpose(0, 4, 1, 3, 2, 5)
        return w.reshape(l, -1, UNITS, P, 2 * width)

    def cols(first, n):
        return w_in[:, :, first:first + n]

    def gate(b, first, n):
        return bodies(cols(C_SILU + b * BW + first * CW, n * CW), CW)

    def rest(b):
        return [bodies(cols(C_MERGE + b * D, D), CW), bodies(w_branch[:, b], CW)]

    wide = [bodies(cols(C_IQ, IDX_HEADS * IDX_DIM), CW), bodies(cols(C_DQ, 3 * BW), CW), gate(DSA, 0, 2), *rest(DSA),
            bodies(cols(C_CQ, 2 * LORA), CW), gate(MLA, 0, 1), bodies(w_kv_up, CW), gate(MLA, 1, 1), *rest(MLA),
            bodies(cols(C_FQ, 3 * BW), CW), gate(FOX, 0, 2), *rest(FOX), bodies(w_out, CW)]
    narrow = np.concatenate([cols(C_IK, N_KPE), cols(C_KPE, ROPE), cols(C_FG, HEADS)], 2)
    return {"w_wide": np.ascontiguousarray(np.concatenate(wide, 1)),
            "w_narrow": np.ascontiguousarray(bodies(narrow, NW)[:, 0]),
            "w_qup": np.ascontiguousarray(bodies(w_q_up, QCW)[:, 0])}


def rope_table(dim):
    half = dim // 2
    inv = np.float32(10000.0) ** (-np.arange(half, dtype=np.float32) / np.float32(half))
    ang = np.arange(SEQ, dtype=np.float32)[:, None] * inv[None, :].astype(np.float32)
    cos, sin = np.cos(ang), np.sin(ang)
    both = np.stack([np.concatenate([cos, cos], 1), np.concatenate([-sin, sin], 1)], 1)
    return np.ascontiguousarray(both.reshape(TT, P, 2, dim).transpose(1, 2, 0, 3).astype(np.float32))


def kernel(**inputs):
    import concourse.bacc as bacc
    from concourse.bass_utils import run_bass_kernel_spmd

    nc = bacc.Bacc("TRN2", target_bir_lowering=False, num_devices=1)
    r = np.arange(P)
    square = np.stack([r[:, None] == r[None, :], r[:, None] <= r[None, :],
                       np.where(r[:, None] < r[None, :], NEG, 0.0)], 1).astype(np.float32)
    given = {n: np.ascontiguousarray(inputs[n]) for n in _INS}
    given.update(weight_units(*(given.pop(n) for n in ("w_in", "w_q_up", "w_kv_up", "w_branch", "w_out"))))
    given["norms_g"] = np.concatenate([given.pop("norm_g"), given["final_norm_g"][None]], 0)
    for n in ("norms_g", "q_norm_g", "kv_norm_g"):
        given[n] = np.ascontiguousarray(given[n].reshape(len(given[n]), -1, P).transpose(0, 2, 1))
    given.update(rope128=rope_table(HD), rope64=rope_table(ROPE), square=square)
    args = {n: nc.dram_tensor(f"in_{n}", a.shape, F32, kind="ExternalInput").ap() for n, a in given.items()}
    out = nc.dram_tensor("out", (1, SEQ, D), F32, kind="ExternalOutput").ap()
    build(nc, out=out, **args)
    r = run_bass_kernel_spmd(nc, [{f"in_{n}": a for n, a in given.items()}], core_ids=[0])
    return r.results[0]["out"]
```
